# Optimizing a Trainium2 kernel written in Bass

```python
import math
import jax, jax.numpy as jnp
from jax import lax
import numpy as np

D_MODEL = 1024
BATCH = 1
SEQ = 2048
DEPTH = 1

CHUNK = 64
Q_BLOCK = 128
EPS = 1e-6
NEG_INF = -1e30

ATT_HEADS = 8
ATT_KV_HEADS = 2
ATT_HEAD_DIM = 64
ATT_Q_WIDTH = ATT_HEADS * ATT_HEAD_DIM
ATT_KV_WIDTH = ATT_KV_HEADS * ATT_HEAD_DIM
IDX_HEADS = 8
IDX_DIM = 32
TOPK_MAX = 256
ROPE_THETA = 500000.0
ROPE_FRACTION = 4

MLSTM_HEADS = 4
MLSTM_HEAD_DIM = 128
MLSTM_WIDTH = MLSTM_HEADS * MLSTM_HEAD_DIM
CONV_WIDTH = 4

N_GROUPS = 4
EXPERTS_PER_GROUP = 8
N_EXPERTS = N_GROUPS * EXPERTS_PER_GROUP
TOP_K_EXPERTS = 2
D_EXPERT = 512
MOE_BLOCK = 128

SPLIT_SIZES = (ATT_Q_WIDTH, ATT_KV_WIDTH, ATT_KV_WIDTH,
               IDX_HEADS * IDX_DIM, IDX_DIM, IDX_HEADS,
               MLSTM_WIDTH, MLSTM_WIDTH, MLSTM_WIDTH, MLSTM_WIDTH,
               MLSTM_HEADS, MLSTM_HEADS,
               D_MODEL, D_MODEL)
D_IN_PROJ = sum(SPLIT_SIZES)

kernel_name = 'hybrid_dsa_mlstm_hmoe_block'

def rmsnorm(x, g):
    xf = x.astype(jnp.float32)
    y = xf * lax.rsqrt(jnp.mean(xf * xf, axis=-1, keepdims=True) + EPS)
    return (y * g.astype(jnp.float32)).astype(x.dtype)

def partial_rope(t, positions):
    d = t.shape[-1]
    rot = d // ROPE_FRACTION
    half = rot // 2
    inv_freq = jnp.float32(ROPE_THETA) ** (-jnp.arange(half, dtype=jnp.float32) * 2.0 / rot)
    ang = positions.astype(jnp.float32)[..., None] * inv_freq
    ang = ang.reshape(ang.shape[:2] + (1,) * (t.ndim - 3) + (half,))
    cos, sin = jnp.cos(ang), jnp.sin(ang)
    t1 = t[..., :half].astype(jnp.float32)
    t2 = t[..., half:rot].astype(jnp.float32)
    rotated = jnp.concatenate([t1 * cos - t2 * sin, t2 * cos + t1 * sin], axis=-1).astype(t.dtype)
    return jnp.concatenate([rotated, t[..., rot:]], axis=-1)

def causal_depthwise_conv(u, w, b):
    c = u.shape[-1]
    y = lax.conv_general_dilated(u, w.astype(u.dtype)[:, None, :], window_strides=(1,),
                                 padding=[(CONV_WIDTH - 1, 0)],
                                 dimension_numbers=('NWC', 'WIO', 'NWC'),
                                 feature_group_count=c)
    return y + b.astype(u.dtype)

def dsa_attention(q, k, v, q_idx, k_idx, w_idx):
    bsz, seq = q.shape[0], q.shape[1]
    groups = ATT_KV_HEADS
    rep = ATT_HEADS // ATT_KV_HEADS
    topk = min(TOPK_MAX, seq // 4)
    nb = seq // Q_BLOCK
    key_chunk = jnp.arange(seq) // CHUNK
    idx_scale = (IDX_DIM * IDX_HEADS) ** -0.5
    att_scale = ATT_HEAD_DIM ** -0.5
    qb = q.reshape(bsz, nb, Q_BLOCK, groups, rep, ATT_HEAD_DIM).swapaxes(0, 1)
    qib = q_idx.reshape(bsz, nb, Q_BLOCK, IDX_HEADS, IDX_DIM).swapaxes(0, 1)
    wib = w_idx.reshape(bsz, nb, Q_BLOCK, IDX_HEADS).swapaxes(0, 1)

    def block(args):
        blk, q_b, qi_b, wi_b = args
        q_chunk = (blk * Q_BLOCK + jnp.arange(Q_BLOCK)) // CHUNK
        visible = key_chunk[None, :] <= q_chunk[:, None]
        rel = jax.nn.relu(jnp.einsum('bqhd,bsd->bqhs', qi_b, k_idx))
        score = jnp.einsum('bqhs,bqh->bqs', rel, wi_b).astype(jnp.float32) * idx_scale
        score = jnp.where(visible[None], score, NEG_INF)
        top_val, top_idx = lax.top_k(score, topk)
        valid = top_val > NEG_INF * 0.5
        k_sel = jax.vmap(lambda kb, ib: kb[ib])(k, top_idx)
        v_sel = jax.vmap(lambda vb, ib: vb[ib])(v, top_idx)
        logits = jnp.einsum('bqgrd,bqkgd->bqgrk', q_b, k_sel).astype(jnp.float32) * att_scale
        logits = jnp.where(valid[:, :, None, None, :], logits, NEG_INF)
        p = jax.nn.softmax(logits, axis=-1)
        return jnp.einsum('bqgrk,bqkgd->bqgrd', p.astype(v.dtype), v_sel)

    out = lax.map(block, (jnp.arange(nb), qb, qib, wib))
    return out.swapaxes(0, 1).reshape(bsz, seq, ATT_Q_WIDTH)

def mlstm_chunkwise(q, k, v, i_pre, f_pre):
    bsz, seq, nh, d = q.shape
    nc = seq // CHUNK

    def to_chunks(t):
        return t.reshape(bsz, nc, CHUNK, nh, d).transpose(1, 0, 3, 2, 4).astype(jnp.float32)

    def gate_chunks(g):
        return g.reshape(bsz, nc, CHUNK, nh).transpose(1, 0, 3, 2)

    q_c = to_chunks(q)
    k_c = to_chunks(k) * (d ** -0.5)
    v_c = to_chunks(v)
    lf_c = gate_chunks(jax.nn.log_sigmoid(f_pre))
    i_c = gate_chunks(i_pre)
    causal = jnp.tril(jnp.ones((CHUNK, CHUNK), dtype=bool))

    def step(carry, inp):
        c_st, n_st, m_st = carry
        qc, kc, vc, lf, ig = inp
        b = jnp.cumsum(lf, axis=-1)
        dmat = jnp.where(causal, b[..., :, None] - b[..., None, :] + ig[..., None, :], NEG_INF)
        inter = b + m_st[..., None]
        m_t = jnp.maximum(inter, jnp.max(dmat, axis=-1))
        w_intra = jnp.exp(dmat - m_t[..., None])
        w_inter = jnp.exp(inter - m_t)
        s = jnp.einsum('bhtd,bhsd->bhts', qc, kc) * w_intra
        num = w_inter[..., None] * jnp.einsum('bhtd,bhde->bhte', qc, c_st) + jnp.einsum('bhts,bhse->bhte', s, vc)
        den = w_inter * jnp.einsum('bhtd,bhd->bht', qc, n_st) + jnp.sum(s, axis=-1)
        h = num / jnp.maximum(jnp.abs(den), jnp.exp(-m_t))[..., None]
        b_last = b[..., -1]
        g = b_last[..., None] - b + ig
        m_new = jnp.maximum(b_last + m_st, jnp.max(g, axis=-1))
        decay = jnp.exp(b_last + m_st - m_new)
        wk = jnp.exp(g - m_new[..., None])
        c_new = decay[..., None, None] * c_st + jnp.einsum('bhs,bhsd,bhse->bhde', wk, kc, vc)
        n_new = decay[..., None] * n_st + jnp.einsum('bhs,bhsd->bhd', wk, kc)
        return (c_new, n_new, m_new), h

    init = (jnp.zeros((bsz, nh, d, d), jnp.float32), jnp.zeros((bsz, nh, d), jnp.float32),
            jnp.zeros((bsz, nh), jnp.float32))
    _, hs = lax.scan(step, init, (q_c, k_c, v_c, lf_c, i_c))
    return hs.transpose(1, 0, 3, 2, 4).reshape(bsz, seq, nh, d).astype(q.dtype)

def routed_experts(xt, expert_id, gate, w_gate, w_up, w_down):
    t, dm = xt.shape
    m = t * TOP_K_EXPERTS
    e_flat = expert_id.reshape(m)
    tok = jnp.arange(m, dtype=jnp.int32) // TOP_K_EXPERTS
    w_flat = gate.reshape(m)
    order = jnp.argsort(e_flat)
    e_sorted = e_flat[order]
    counts = jax.ops.segment_sum(jnp.ones((m,), jnp.int32), e_flat, num_segments=N_EXPERTS)
    padded = ((counts + MOE_BLOCK - 1) // MOE_BLOCK) * MOE_BLOCK
    starts = jnp.cumsum(counts) - counts
    pends = jnp.cumsum(padded)
    pstarts = pends - padded
    dest = pstarts[e_sorted] + (jnp.arange(m, dtype=jnp.int32) - starts[e_sorted])
    total = ((m + N_EXPERTS * MOE_BLOCK + MOE_BLOCK - 1) // MOE_BLOCK) * MOE_BLOCK
    nblk = total // MOE_BLOCK
    buf_tok = jnp.zeros((total,), jnp.int32).at[dest].set(tok[order])
    buf_w = jnp.zeros((total,), xt.dtype).at[dest].set(w_flat[order])
    block_e = jnp.minimum(jnp.searchsorted(pends, jnp.arange(nblk) * MOE_BLOCK, side='right'),
                          N_EXPERTS - 1)
    xb = xt[buf_tok].reshape(nblk, MOE_BLOCK, dm)

    def expert_block(args):
        xblk, e = args
        hid = jax.nn.silu(xblk @ w_gate[e]) * (xblk @ w_up[e])
        return hid @ w_down[e]

    yb = lax.map(expert_block, (xb, block_e)).reshape(total, dm)
    return jnp.zeros((t, dm), xt.dtype).at[buf_tok].add(yb * buf_w[:, None])

def hierarchical_moe(xn, w_router_group, b_router_group, w_router_expert, b_router_expert,
                     w_exp_gate, w_exp_up, w_exp_down):
    bsz, seq, dm = xn.shape
    xt = xn.reshape(bsz * seq, dm)
    g_logits = (xt @ w_router_group).astype(jnp.float32) + b_router_group.astype(jnp.float32)
    g_prob = jax.nn.softmax(g_logits, axis=-1)
    g_top_val, g_sel = lax.top_k(g_prob, 1)
    e_logits = ((xt @ w_router_expert).astype(jnp.float32) + b_router_expert.astype(jnp.float32))
    e_logits = e_logits.reshape(-1, N_GROUPS, EXPERTS_PER_GROUP)
    in_group = jnp.take_along_axis(e_logits, g_sel[:, :, None], axis=1)[:, 0]
    top_val, top_loc = lax.top_k(in_group, TOP_K_EXPERTS)
    gate = (jax.nn.softmax(top_val, axis=-1) * g_top_val).astype(xt.dtype)
    expert_id = g_sel * EXPERTS_PER_GROUP + top_loc
    y = routed_experts(xt, expert_id, gate, w_exp_gate, w_exp_up, w_exp_down)
    return y.reshape(bsz, seq, dm)

def hybrid_layer(x, positions, g_norm_mix, w_in, g_q_att, g_k_att, w_conv_mlstm, b_conv_mlstm,
                 b_igate, b_fgate, g_norm_mlstm_out, w_proj_att, w_proj_mlstm, w_out,
                 g_norm_moe, w_router_group, b_router_group, w_router_expert, b_router_expert,
                 w_exp_gate, w_exp_up, w_exp_down):
    bsz, seq, _ = x.shape
    h = rmsnorm(x, g_norm_mix)
    proj = h @ w_in
    points = np.cumsum(SPLIT_SIZES)[:-1].tolist()
    (aq, ak, av, iq, ik, iw, mq, mk, mv, mo, mi, mf, ga, gm) = jnp.split(proj, points, axis=-1)

    aq = partial_rope(rmsnorm(aq.reshape(bsz, seq, ATT_HEADS, ATT_HEAD_DIM), g_q_att), positions)
    ak = partial_rope(rmsnorm(ak.reshape(bsz, seq, ATT_KV_HEADS, ATT_HEAD_DIM), g_k_att), positions)
    av = av.reshape(bsz, seq, ATT_KV_HEADS, ATT_HEAD_DIM)
    iq = partial_rope(iq.reshape(bsz, seq, IDX_HEADS, IDX_DIM), positions)
    ik = partial_rope(ik, positions)
    y_att = dsa_attention(aq, ak, av, iq, ik, iw)

    qk = jax.nn.silu(causal_depthwise_conv(jnp.concatenate([mq, mk], axis=-1), w_conv_mlstm, b_conv_mlstm))
    mq, mk = jnp.split(qk, 2, axis=-1)
    shp = (bsz, seq, MLSTM_HEADS, MLSTM_HEAD_DIM)
    i_pre = mi.astype(jnp.float32) + b_igate.astype(jnp.float32)
    f_pre = mf.astype(jnp.float32) + b_fgate.astype(jnp.float32)
    hm = mlstm_chunkwise(mq.reshape(shp), mk.reshape(shp), mv.reshape(shp), i_pre, f_pre)
    hm = rmsnorm(hm, g_norm_mlstm_out.reshape(MLSTM_HEADS, MLSTM_HEAD_DIM)).reshape(bsz, seq, MLSTM_WIDTH)
    y_mlstm = jax.nn.sigmoid(mo) * hm

    merged = jax.nn.sigmoid(ga) * (y_att @ w_proj_att) + jax.nn.sigmoid(gm) * (y_mlstm @ w_proj_mlstm)
    x = x + merged @ w_out

    xn = rmsnorm(x, g_norm_moe)
    return x + hierarchical_moe(xn, w_router_group, b_router_group, w_router_expert, b_router_expert,
                                w_exp_gate, w_exp_up, w_exp_down)

def setup_inputs(seed: int = 0) -> dict:
    key = jax.random.key(seed)
    ks = jax.random.split(key, 24)
    L = DEPTH

    def nrm(k, shape, fan_in):
        return jax.random.normal(k, shape, jnp.float32) * (fan_in ** -0.5)

    def gain(k, shape):
        return 1.0 + 0.02 * jax.random.normal(k, shape, jnp.float32)

    def small(k, shape, scale):
        return scale * jax.random.normal(k, shape, jnp.float32)

    x = jax.random.normal(ks[0], (BATCH, SEQ, D_MODEL), jnp.float32)
    offsets = jax.random.randint(ks[1], (BATCH, 1), 0, 100000, dtype=jnp.int32)
    positions = (offsets + jnp.arange(SEQ, dtype=jnp.int32)[None, :]).astype(jnp.int32)
    return {
        'x': x,
        'positions': positions,
        'g_norm_mix': gain(ks[2], (L, D_MODEL)),
        'w_in': nrm(ks[3], (L, D_MODEL, D_IN_PROJ), D_MODEL),
        'g_q_att': gain(ks[4], (L, ATT_HEAD_DIM)),
        'g_k_att': gain(ks[5], (L, ATT_HEAD_DIM)),
        'w_conv_mlstm': nrm(ks[6], (L, CONV_WIDTH, 2 * MLSTM_WIDTH), CONV_WIDTH),
        'b_conv_mlstm': small(ks[7], (L, 2 * MLSTM_WIDTH), 0.01),
        'b_igate': -1.0 + small(ks[8], (L, MLSTM_HEADS), 0.1),
        'b_fgate': 3.0 + small(ks[9], (L, MLSTM_HEADS), 0.5),
        'g_norm_mlstm_out': gain(ks[10], (L, MLSTM_WIDTH)),
        'w_proj_att': nrm(ks[11], (L, ATT_Q_WIDTH, D_MODEL), ATT_Q_WIDTH),
        'w_proj_mlstm': nrm(ks[12], (L, MLSTM_WIDTH, D_MODEL), MLSTM_WIDTH),
        'w_out': nrm(ks[13], (L, D_MODEL, D_MODEL), D_MODEL),
        'g_norm_moe': gain(ks[14], (L, D_MODEL)),
        'w_router_group': nrm(ks[15], (L, D_MODEL, N_GROUPS), D_MODEL),
        'b_router_group': small(ks[16], (L, N_GROUPS), 0.01),
        'w_router_expert': nrm(ks[17], (L, D_MODEL, N_EXPERTS), D_MODEL),
        'b_router_expert': small(ks[18], (L, N_EXPERTS), 0.01),
        'w_exp_gate': nrm(ks[19], (L, N_EXPERTS, D_MODEL, D_EXPERT), D_MODEL),
        'w_exp_up': nrm(ks[20], (L, N_EXPERTS, D_MODEL, D_EXPERT), D_MODEL),
        'w_exp_down': nrm(ks[21], (L, N_EXPERTS, D_EXPERT, D_MODEL), D_EXPERT),
    }

def reference(x, positions, g_norm_mix, w_in, g_q_att, g_k_att, w_conv_mlstm, b_conv_mlstm,
              b_igate, b_fgate, g_norm_mlstm_out, w_proj_att, w_proj_mlstm, w_out,
              g_norm_moe, w_router_group, b_router_group, w_router_expert, b_router_expert,
              w_exp_gate, w_exp_up, w_exp_down):
    for l in range(DEPTH):
        x = hybrid_layer(x, positions, g_norm_mix[l], w_in[l], g_q_att[l], g_k_att[l],
                         w_conv_mlstm[l], b_conv_mlstm[l], b_igate[l], b_fgate[l],
                         g_norm_mlstm_out[l], w_proj_att[l], w_proj_mlstm[l], w_out[l],
                         g_norm_moe[l], w_router_group[l], b_router_group[l],
                         w_router_expert[l], b_router_expert[l],
                         w_exp_gate[l], w_exp_up[l], w_exp_down[l])
    return x


_drawn_inputs = setup_inputs


def setup_inputs(seed=0):
    import zlib

    import numpy as np

    out = dict(_drawn_inputs(seed))
    spreads = {}
    factors = {'g_q_att': 8.0,
     'g_k_att': 8.0,
     'b_conv_mlstm': 6.225,
     'b_igate': 8.0,
     'g_norm_mlstm_out': 11.016,
     'b_router_group': 20.476,
     'b_router_expert': 13.482,
     'g_norm_moe': 3.732}
    for name, (base, spread) in spreads.items():
        noise = np.random.default_rng([zlib.crc32(name.encode()), seed]).standard_normal(out[name].shape)
        drawn = base * np.exp(spread * noise) if base else spread * noise
        out[name] = __import__('jax').numpy.asarray(drawn.astype(out[name].dtype))
    for name, factor in factors.items():
        out[name] = (out[name] * factor).astype(out[name].dtype)
    return out
```

```python
from contextlib import ExitStack

import concourse.bass as bass
from concourse import mybir
import numpy as np

F32 = mybir.dt.float32
F32R = mybir.dt.float32r
BF16 = mybir.dt.bfloat16
I32 = mybir.dt.int32
U32 = mybir.dt.uint32
ALU = mybir.AluOpType
ACT = mybir.ActivationFunctionType
AX = mybir.AxisListType

P = 128
SEQ, DM = 2048, 1024
NT = SEQ // P
KT = DM // P
NCH = SEQ // 512
EPS = 1e-6
ROPE_THETA = 500000.0
NEG = -1e30
AH, AKV, AD = 8, 2, 64
IH, ID = 8, 32
TOPK = 256
CONV = 4
MH, MD = 4, 128
NG, EG, DE = 4, 8, 512
NE = NG * EG
W_A = AH * AD + 2 * AKV * AD + IH * ID + ID + IH
C_MQK = W_A
C_MV = C_MQK + 2 * MH * MD
C_MO = C_MV + MH * MD
C_IF = C_MO + MH * MD
C_GA = C_IF + 2 * MH
D_IN = C_GA + 2 * DM
CT = -(-D_IN // P)
NBLK = 63
SLOTS = NBLK * P
USED, LAST, EMPTY = NBLK + 2, NBLK + 3, NBLK + 4


class Steps:

    def __init__(self, eng, sem):
        self.eng, self.sem, self.done, self.at, self.k = eng, sem, 0, 0, 0

    def __call__(self, ins):
        ins.then_inc(self.sem, 1)
        self.k += 1
        self.eng.wait_ge(self.sem, self.at + (self.done + self.k))

    def body(self, at):
        self.at, self.k = at, 0

    def end(self, trips, per):
        assert self.k == per, (self.k, per)
        self.done, self.at, self.k = self.done + trips * per, 0, 0


class Prog:
    def __init__(self, nc, ins, scratch_kind="Internal"):
        self.nc, self.i = nc, ins
        self.d = {}
        self.kind = scratch_kind

    def sw_sem(self, name):
        return self.nc.alloc_semaphore(name)

    def semaphores(self, c, prefix=""):
        nc, held = self.nc, []

        def release():
            nc.clear_and_free_semaphores(held)
            nc.all_engine_barrier()

        def sem(name):
            held.append(nc.alloc_semaphore(prefix + name))
            return held[-1]
        c.callback(release)
        return sem

    def dram(self, name, shape, dt=F32):
        kw = {} if self.kind == "Internal" else {"kind": self.kind}
        self.d[name] = self.nc.dram_tensor(name, shape, dt, **kw).ap()
        return self.d[name]


def hold(eng, held):
    eng.sem_inc(held, 1)


def identity(nc, pool, tile, sem):
    nc.gpsimd.memset(tile, 0.0).then_inc(sem, 1)
    pool.wait_ge(sem, 1)
    nc.gpsimd.affine_select(out=tile, in_=tile, compare_op=ALU.not_equal, fill=1.0, base=0,
                            pattern=[[-1, P]], channel_multiplier=1).then_inc(sem, 1)


def project_in(pg):
    nc, i = pg.nc, pg.i
    proj = pg.dram("projT", (CT * P, SEQ))
    with ExitStack() as c:
        sb = lambda n, s, d=F32: c.enter_context(nc.sbuf_tensor(n, s, d))
        sem = pg.semaphores(c)
        h_hi = sb("h_hi", [P, KT, SEQ], F32R)
        h_lo = sb("h_lo", [P, KT, SEQ], F32R)
        consts, ident_ok = sem("p1_consts"), sem("p1_ident")
        x_loaded = [sem(f"x_loaded{b}") for b in range(2)]
        sq_done, rt_done, h_done, tr_done, hi_done, lo_done = (sem(n) for n in (
            "p1_sq", "p1_rt", "p1_h", "p1_tr", "p1_hi", "p1_lo"))
        v_own = sem("p1_v")
        with ExitStack() as c1:
            sb1 = lambda n, s, d=F32: c1.enter_context(nc.sbuf_tensor(n, s, d))
            x_t = sb1("x_t", [P, 2, DM])
            h_t = sb1("h_t", [P, 2, DM])
            junk = sb1("p1_junk", [P, DM])
            gain = sb1("gain_mix", [P, DM])
            ident = sb1("ident1", [P, P])
            eps = sb1("eps1", [P, 1])
            ss = sb1("p1_ss", [P, 2])
            rt = sb1("p1_rms", [P, 2])
            rs = sb1("p1_rstd", [P, 2])
            pt = c1.enter_context(nc.psum_tensor("p1_pt", [P, 2, KT, P], F32))
            block = c1.enter_context(nc.Block())

            @block.sync
            def _(sp):
                sp.dma_start(gain[:, :], i["g_norm_mix"].partition_broadcast(P)).then_inc(consts, 16)
                with sp.Fori(0, NT // 2) as t:
                    for b in range(2):
                        sp.wait_ge(h_done, 2 * t)
                        sp.dma_start(x_t[:, b, :], i["x"][bass.ds((2 * t + b) * P, P), :]).then_inc(x_loaded[b], 16)

            @block.gpsimd
            def _(pool):
                identity(nc, pool, ident[:, :], ident_ok)
                nc.gpsimd.memset(eps[:, :], EPS).then_inc(ident_ok, 1)

            @block.scalar
            def _(act):
                act.wait_ge(ident_ok, 3)
                with act.Fori(0, NT // 2) as t:
                    for b in range(2):
                        act.wait_ge(x_loaded[b], 16 * t + 16)
                        act.wait_ge(rt_done, 2 * t + b)
                        nc.scalar.activation(junk[:, :], x_t[:, b, :], ACT.Square, accum_out=ss[:, b:b + 1]).then_inc(sq_done, 1)
                        act.wait_ge(sq_done, 2 * t + b + 1)
                        act.wait_ge(h_done, 2 * t)
                        nc.scalar.activation(rt[:, b:b + 1], ss[:, b:b + 1], ACT.Sqrt, bias=eps[:, :], scale=1.0 / DM).then_inc(rt_done, 1)
                    for b in range(2):
                        act.wait_ge(tr_done, 2 * t + b + 1)
                        nc.scalar.copy(h_hi[:, :, bass.ds((2 * t + b) * P, P)], pt[:, b, :, :]).then_inc(hi_done, 1)

            @block.vector
            def _(dve):
                own = Steps(dve, v_own)
                dve.wait_ge(consts, 16)
                with dve.Fori(0, NT // 2) as t:
                    own.body(t * 2)
                    for b in range(2):
                        dve.wait_ge(rt_done, 2 * t + b + 1)
                        own(nc.vector.reciprocal(rs[:, b:b + 1], rt[:, b:b + 1]))
                        dve.wait_ge(tr_done, 2 * t)
                        nc.vector.scalar_tensor_tensor(out=h_t[:, b, :], in0=x_t[:, b, :], scalar=rs[:, b:b + 1],
                                                       in1=gain[:, :], op0=ALU.mult, op1=ALU.mult).then_inc(h_done, 1)
                    for b in range(2):
                        dve.wait_ge(hi_done, 2 * t + b + 1)
                        at = bass.ds((2 * t + b) * P, P)
                        nc.vector.tensor_tensor(h_lo[:, :, at], pt[:, b, :, :], h_hi[:, :, at].bitcast(F32),
                                                ALU.subtract).then_inc(lo_done, 1)
                    
                own.end(NT // 2, 2)

            @block.tensor
            def _(pe):
                pe.wait_ge(ident_ok, 3)
                with pe.Fori(0, NT // 2) as t:
                    for b in range(2):
                        pe.wait_ge(h_done, 2 * t + b + 1)
                        pe.wait_ge(lo_done, 2 * t)
                        for k in range(KT):
                            last = nc.tensor.transpose(pt[:, b, k, :], h_t[:, b, k * P:(k + 1) * P], ident[:, :])
                        last.then_inc(tr_done, 1)

        with ExitStack() as c2:
            sb2 = lambda n, s, d=F32: c2.enter_context(nc.sbuf_tensor(n, s, d))
            w_raw = sb2("w_raw", [P, 2, KT, P])
            w_hi = sb2("w_hi", [P, 2, KT, P], F32R)
            w_lo = sb2("w_lo", [P, 2, KT, P], F32R)
            out_t = sb2("proj_t", [P, 2, SEQ])
            ps = c2.enter_context(nc.psum_tensor("p2_ps", [P, 2, NCH, 512], F32))
            w_split_hi, w_split_lo, mm_done, ev_act, ev_dve = (sem(n) for n in (
                "p2_hi", "p2_lo", "p2_mm", "p2_eva", "p2_evv"))
            w_loaded = [sem(f"w_in_loaded{b}") for b in range(2)]
            stored = [pg.sw_sem(f"proj_stored{b}") for b in range(2)]
            block = c2.enter_context(nc.Block())
            LAST = CT - 1
            WL = D_IN - LAST * P
            PAIRS = LAST // 2
            assert LAST % 2 == 0
            w_v = i["w_in"].rearrange("(k p) n -> p k n", p=P)

            def each(eng, f):
                with eng.Fori(0, PAIRS) as t:
                    for b in range(2):
                        f(t, b, P)
                f(PAIRS, 0, WL)

            @block.sync
            def _(sp):
                def load(t, b, w):
                    sp.wait_ge(w_split_lo, 2 * t)
                    sp.dma_start(w_raw[:, b, :, 0:w], w_v[:, :, bass.ds((2 * t + b) * P, w)]).then_inc(w_loaded[b], 16)
                each(sp, load)

            @block.scalar
            def _(act):
                def step(t, b, w):
                    act.wait_ge(w_loaded[b], 16 * t + 16)
                    act.wait_ge(mm_done, 2 * t)
                    nc.scalar.copy(w_hi[:, b, :, 0:w], w_raw[:, b, :, 0:w]).then_inc(w_split_hi, 1)
                def out(t, b, w):
                    act.wait_ge(mm_done, 2 * t + b + 1)
                    act.wait_ge(stored[b], 16 * t)
                    nc.scalar.copy(out_t[0:w, b, 0:SEQ // 2], ps[0:w, b, 0:2, :].rearrange("p a n -> p (a n)")).then_inc(ev_act, 1)
                with act.Fori(0, PAIRS) as t:
                    for b in range(2):
                        step(t, b, P)
                    for b in range(2):
                        out(t, b, P)
                step(PAIRS, 0, WL)
                out(PAIRS, 0, WL)

            @block.vector
            def _(dve):
                def step(t, b, w):
                    dve.wait_ge(w_split_hi, 2 * t + b + 1)
                    nc.vector.tensor_tensor(w_lo[:, b, :, 0:w], w_raw[:, b, :, 0:w], w_hi[:, b, :, 0:w].bitcast(F32),
                                            ALU.subtract).then_inc(w_split_lo, 1)
                def out(t, b, w):
                    dve.wait_ge(mm_done, 2 * t + b + 1)
                    dve.wait_ge(stored[b], 16 * t)
                    nc.vector.tensor_copy(out_t[0:w, b, SEQ // 2:SEQ], ps[0:w, b, 2:4, :].rearrange("p a n -> p (a n)")).then_inc(ev_dve, 1)
                with dve.Fori(0, PAIRS) as t:
                    for b in range(2):
                        step(t, b, P)
                    for b in range(2):
                        out(t, b, P)
                step(PAIRS, 0, WL)
                out(PAIRS, 0, WL)

            @block.tensor
            def _(pe):
                def mm(t, b, w):
                    pe.wait_ge(w_split_lo, 2 * t + b + 1)
                    pe.wait_ge(ev_act, 2 * t)
                    pe.wait_ge(ev_dve, 2 * t)
                    for k in range(KT):
                        for s, (wt, ht) in enumerate(((w_hi, h_hi), (w_hi, h_lo), (w_lo, h_hi))):
                            for q in range(NCH):
                                last = nc.tensor.matmul(ps[0:w, b, q, :], wt[:, b, k, 0:w], ht[:, k, q * 512:(q + 1) * 512],
                                                        start=(k == 0 and s == 0), stop=(k == KT - 1 and s == 2))
                    last.then_inc(mm_done, 1)
                each(pe, mm)

            @block.gpsimd
            def _(pool):
                def store(t, b, w):
                    pool.wait_ge(ev_act, 2 * t + b + 1)
                    pool.wait_ge(ev_dve, 2 * t + b + 1)
                    pool.dma_start(proj[bass.ds((2 * t + b) * P, w), :], out_t[0:w, b, :]).then_inc(stored[b], 16)
                each(pool, store)
                for b in range(2):
                    pool.wait_ge(stored[b], 16 * (PAIRS + 1 - b))


def rope_freqs():
    return [float(np.float32(np.float64(ROPE_THETA) ** (-2.0 * j / 16))) for j in range(8)]


def over_heads(ap, n):
    return ap.broadcast_to([ap.shape[0], n, ap.shape[2]])


def attention_operands(pg):
    nc, i = pg.nc, pg.i
    proj = pg.d["projT"]
    qs_d = pg.dram("q_stack", (NT, P, AH * 2 * P))
    ks_d = pg.dram("k_stack", (P, AKV, SEQ))
    iqs_d = pg.dram("iq_stack", (NT, P, IH * P))
    iks_d = pg.dram("ik_stack", (P, SEQ))
    v_d = pg.dram("v", (P, NT, AKV, AD))
    iw_d = pg.dram("iw", (P, NT, IH))
    NQ = AH * AD
    NQK = NQ + AKV * AD
    NV = NQK + AKV * AD
    NI = (IH + 1) * ID
    HH = AH + AKV
    with ExitStack() as c:
        sb = lambda n, s, d=F32: c.enter_context(nc.sbuf_tensor(n, s, d))
        sem = pg.semaphores(c)
        a_t = sb("a_t", [P, 2, 9, P])
        T = sb("a_tok", [P, 1152])
        sq = sb("a_sq", [P, NQK])
        ms, rms, rstd = (sb(n, [P, HH]) for n in ("a_ms", "a_rms", "a_rstd"))
        N = sb("a_norm", [P, NQK])
        G = sb("a_gain", [P, NQK])
        gq, gk = sb("a_gq", [P, 1, AD]), sb("a_gk", [P, 1, AD])
        r1, r2, r3, r4 = (sb(f"a_r{n}", [P, HH, 8]) for n in range(4))
        j1, j2, j3, j4 = (sb(f"a_j{n}", [P, IH + 1, 4]) for n in range(4))
        QHL = sb("a_qhl", [P, AH, 2, 2, AD], F32R)
        KHL = sb("a_khl", [P, AKV, 2, AD], F32R)
        IHL = sb("a_ihl", [P, IH, 2, 2, ID], F32R)
        IKL = sb("a_ikl", [P, 2, 2, ID], F32R)
        QS = sb("a_qs", [P, AH * 2 * P], F32R)
        KI = sb("a_ki", [P, 11, P], F32R)
        V = sb("a_v", [P, NT, AKV, AD])
        IW = sb("a_iw", [P, NT, IH])
        ident = sb("ident3", [P, P])
        eps = sb("eps3", [P, 1])
        pos_i = sb("pos_i", [P, NT], I32)
        pos = sb("pos", [P, NT])
        ang, kk, kh, kl, cos, sin = (sb(n, [P, NT, 8]) for n in ("ang", "turns", "turns_h", "turns_l", "cos", "sin"))
        psT = c.enter_context(nc.psum_tensor("a_psT", [P, 1536], F32))
        psQ = c.enter_context(nc.psum_tensor("a_psQ", [P, AH * 2 * P], F32))
        loaded = [sem(f"a_loaded{b}") for b in range(2)]
        held = sem("a_held")
        vw_st = pg.sw_sem("vw_st")
        (consts, setup, sin_arg, sin_ok, cos_ok, tok_ps, tok_ok, sq_ok, ms_ok, rms_ok, norm_ok, hi_ok, lo_ok, ilo_ok, vw_ok,
         q_ps, ki_ps, q_ev, ki_ev, q_st, k_st, i_st, ik_st, v_own, p_own) = (sem("a_" + n) for n in (
            "consts", "setup", "sin_arg", "sin_ok", "cos_ok", "tok_ps", "tok_ok", "sq_ok", "ms_ok", "rms_ok", "norm_ok",
            "hi_ok", "lo_ok", "ilo_ok", "vw_ok", "q_ps", "ki_ps", "q_ev", "ki_ev", "q_st", "k_st", "i_st", "ik_st",
            "v_own", "p_own"))
        block = c.enter_context(nc.Block())

        @block.sync
        def _(sp):
            sp.dma_start(pos_i[:, :], i["positions"]).then_inc(consts, 16)
            sp.dma_start(gq[:, 0, :], i["g_q_att"].partition_broadcast(P)).then_inc(consts, 16)
            sp.dma_start(gk[:, 0, :], i["g_k_att"].partition_broadcast(P)).then_inc(consts, 16)
            for b in range(2):
                sp.dma_start(a_t[:, b, :, :], proj[0:9 * P, b * P:b * P + P].rearrange("(c p) n -> p c n", p=P)
                             ).then_inc(loaded[b], 16)
            with sp.Fori(0, NT // 2) as t:
                for b in range(2):
                    n = 2 * t + b
                    sp.wait_ge(q_ev, n + 1)
                    sp.dma_start(qs_d[bass.ds(n, 1)].rearrange("o p n -> (o p) n"), QS[:, :].bitcast(F32)).then_inc(q_st, 16)
                    sp.wait_ge(ki_ev, n + 1)
                    sp.dma_start(ks_d[:, :, bass.ds(n * P, P)], KI[:, 0:2, :].bitcast(F32)).then_inc(k_st, 16)
                    sp.dma_start(iqs_d[bass.ds(n, 1)].rearrange("o p n -> (o p) n"),
                                 KI[:, 2:10, :].bitcast(F32).rearrange("p h n -> p (h n)")).then_inc(i_st, 16)
                    sp.dma_start(iks_d[:, bass.ds(n * P, P)], KI[:, 10, :].bitcast(F32)).then_inc(ik_st, 16)
                    sp.wait_ge(tok_ps, n + 1)
                    sp.dma_start(a_t[:, b, :, :], proj[0:9 * P, bass.ds(((n + 2) % NT) * P, P)]
                                 .rearrange("(c p) n -> p c n", p=P)).then_inc(loaded[b], 16)
            for s in (q_st, k_st, i_st, ik_st):
                sp.wait_ge(s, 16 * NT)
            for b in range(2):
                sp.wait_ge(loaded[b], 16 * (NT // 2 + 1))

        @block.gpsimd
        def _(pool):
            identity(nc, pool, ident[:, :], setup)
            nc.gpsimd.memset(eps[:, :], EPS).then_inc(setup, 1)
            pool.wait_ge(sin_ok, 1)
            pool.wait_ge(cos_ok, 1)
            own = Steps(pool, p_own)
            with pool.Fori(0, NT) as t:
                own.body(t * 4)
                X = T[:, NV:NV + NI].rearrange("p (h d) -> p h d", d=ID)
                x1, x2 = X[:, :, 0:4], X[:, :, 4:8]
                cs, sn = (over_heads(z[:, bass.ds(t, 1), 0:8:2], IH + 1) for z in (cos, sin))
                pool.wait_ge(tok_ok, t + 1)
                nc.gpsimd.tensor_tensor(j1[:, :, :], x1, cs, ALU.mult)
                nc.gpsimd.tensor_tensor(j2[:, :, :], x2, sn, ALU.mult)
                nc.gpsimd.tensor_tensor(j3[:, :, :], x2, cs, ALU.mult)
                own(nc.gpsimd.tensor_tensor(j4[:, :, :], x1, sn, ALU.mult))
                nc.gpsimd.tensor_tensor(x1, j1[:, :, :], j2[:, :, :], ALU.subtract)
                own(nc.gpsimd.tensor_tensor(x2, j3[:, :, :], j4[:, :, :], ALU.add))
                pool.wait_ge(ki_ps, t)
                hold(pool, held)
                iq = X[:, 0:IH, :].unsqueeze(2).broadcast_to([P, IH, 2, ID])
                ik = X[:, IH:IH + 1, :].broadcast_to([P, 2, ID])
                nc.gpsimd.tensor_copy(IHL[:, :, 0, :, :], iq)
                own(nc.gpsimd.tensor_copy(IKL[:, :, 0, :], ik))
                nc.gpsimd.tensor_tensor(IHL[:, :, 1, :, :], iq, IHL[:, :, 0, :, :].bitcast(F32), ALU.subtract)
                own(nc.gpsimd.tensor_tensor(IKL[:, :, 1, :], ik, IKL[:, :, 0, :].bitcast(F32), ALU.subtract))
                nc.gpsimd.tensor_copy(V[:, bass.ds(t, 1), :, :], T[:, NQK:NV].rearrange("p (a g d) -> p a g d", a=1, d=AD))
                nc.gpsimd.tensor_copy(IW[:, bass.ds(t, 1), :], T[:, NV + NI:W_A].rearrange("p (a d) -> p a d", a=1)).then_inc(ilo_ok, 1)
            pool.wait_ge(ilo_ok, NT)
            pool.dma_start(v_d, V[:, :, :, :]).then_inc(vw_st, 16)
            pool.dma_start(iw_d, IW[:, :, :]).then_inc(vw_st, 16)
            pool.wait_ge(vw_st, 32)

        @block.scalar
        def _(act):
            act.wait_ge(setup, 3)
            act.wait_ge(sin_arg, 1)
            nc.scalar.activation(sin[:, :, :], ang[:, :, :], ACT.Sin).then_inc(sin_ok, 1)
            nc.scalar.activation(kh[:, :, :], ang[:, :, :], ACT.Sin, scale=0.5).then_inc(sin_ok, 1)
            with act.Fori(0, NT) as t:
                act.wait_ge(tok_ps, t + 1)
                act.wait_ge(norm_ok, t)
                act.wait_ge(ilo_ok, t)
                nc.scalar.copy(T[:, :], psT[:, 0:1152]).then_inc(tok_ok, 1)
                act.wait_ge(tok_ok, t + 1)
                nc.scalar.activation(sq[:, :], T[:, 0:NQK], ACT.Square).then_inc(sq_ok, 1)
                act.wait_ge(ms_ok, t + 1)
                nc.scalar.activation(rms[:, :], ms[:, :], ACT.Sqrt, bias=eps[:, :], scale=1.0 / AD).then_inc(rms_ok, 1)
                act.wait_ge(norm_ok, t + 1)
                act.wait_ge(ki_ps, t)
                X = N[:, :].rearrange("p (h d) -> p h d", d=AD)
                nc.scalar.copy(QHL[:, :, 0, :, :], X[:, 0:AH, :].unsqueeze(2).broadcast_to([P, AH, 2, AD]))
                nc.scalar.copy(KHL[:, :, 0, :], X[:, AH:HH, :]).then_inc(hi_ok, 1)
                act.wait_ge(q_ps, t + 1)
                act.wait_ge(q_st, 16 * t)
                nc.scalar.copy(QS[:, :], psQ[:, :]).then_inc(q_ev, 1)

        @block.vector
        def _(dve):
            own = Steps(dve, v_own)
            dve.wait_ge(consts, 48)
            own(nc.vector.tensor_copy(pos[:, :], pos_i[:, :]))
            for j, f in enumerate(rope_freqs()):
                last = nc.vector.tensor_scalar(ang[:, :, j], pos[:, :], f, None, ALU.mult)
            own(last)
            MAGIC, T1, T2 = 12582912.0, 6.28125, 2029 / 2.0 ** 20
            T3 = float(2 * np.pi - T1 - T2)
            A, K, KH, KL = ang[:, :, :], kk[:, :, :], kh[:, :, :], kl[:, :, :]
            own(nc.vector.tensor_scalar(K, A, 1 / (2 * np.pi), MAGIC, ALU.mult, ALU.add))
            own(nc.vector.tensor_scalar(K, K, MAGIC, None, ALU.subtract))
            own(nc.vector.tensor_scalar(KH, K, 1 / 2048, MAGIC, ALU.mult, ALU.add))
            own(nc.vector.tensor_scalar(KH, KH, MAGIC, 2048.0, ALU.subtract, ALU.mult))
            own(nc.vector.tensor_tensor(KL, K, KH, ALU.subtract))
            for part, turn in ((KH, T1), (KL, T1), (KH, T2), (KL, T2), (K, T3)):
                own(nc.vector.scalar_tensor_tensor(out=A, in0=part, scalar=-turn, in1=A, op0=ALU.mult, op1=ALU.add))
            nc.vector.tensor_scalar(A, A, 3.1415925, -3.1415925, ALU.min, ALU.max).then_inc(sin_arg, 1)
            dve.wait_ge(sin_ok, 2)
            own(nc.vector.tensor_tensor(K, KH, KH, ALU.mult))
            nc.vector.tensor_scalar(cos[:, :, :], K, -2.0, 1.0, ALU.mult, ALU.add).then_inc(cos_ok, 1)
            gv = G[:, :].rearrange("p (h d) -> p h d", d=AD)
            nc.vector.tensor_scalar(gv[:, 0:AH, :], over_heads(gq[:, :, :], AH), AD ** -0.5, None, ALU.mult)
            own(nc.vector.tensor_copy(gv[:, AH:HH, :], over_heads(gk[:, :, :], AKV)))
            dve.wait_ge(cos_ok, 1)
            own.end(1, own.k)
            with dve.Fori(0, NT) as t:
                own.body(t * 4)
                dve.wait_ge(sq_ok, t + 1)
                nc.vector.tensor_reduce(ms[:, :], sq[:, :].rearrange("p (h d) -> p h d", d=AD), AX.X, ALU.add).then_inc(ms_ok, 1)
                dve.wait_ge(rms_ok, t + 1)
                own(nc.vector.reciprocal(rstd[:, :], rms[:, :]))
                X = N[:, :].rearrange("p (h d) -> p h d", d=AD)
                own(nc.vector.tensor_tensor(X, T[:, 0:NQK].rearrange("p (h d) -> p h d", d=AD),
                                            rstd[:, :].unsqueeze(2).broadcast_to([P, HH, AD]), ALU.mult))
                own(nc.vector.tensor_tensor(N[:, :], N[:, :], G[:, :], ALU.mult))
                x1, x2 = X[:, :, 0:8], X[:, :, 8:16]
                cs, sn = (over_heads(z[:, bass.ds(t, 1), :], HH) for z in (cos, sin))
                nc.vector.tensor_tensor(r1[:, :, :], x1, cs, ALU.mult)
                nc.vector.tensor_tensor(r2[:, :, :], x2, sn, ALU.mult)
                nc.vector.tensor_tensor(r3[:, :, :], x2, cs, ALU.mult)
                own(nc.vector.tensor_tensor(r4[:, :, :], x1, sn, ALU.mult))
                nc.vector.tensor_tensor(x1, r1[:, :, :], r2[:, :, :], ALU.subtract)
                nc.vector.tensor_tensor(x2, r3[:, :, :], r4[:, :, :], ALU.add).then_inc(norm_ok, 1)
                dve.wait_ge(hi_ok, t + 1)
                nc.vector.tensor_tensor(QHL[:, :, 1, :, :], X[:, 0:AH, :].unsqueeze(2).broadcast_to([P, AH, 2, AD]),
                                        QHL[:, :, 0, :, :].bitcast(F32), ALU.subtract)
                nc.vector.tensor_tensor(KHL[:, :, 1, :], X[:, AH:HH, :], KHL[:, :, 0, :].bitcast(F32),
                                        ALU.subtract).then_inc(lo_ok, 1)
                dve.wait_ge(ki_ps, t + 1)
                dve.wait_ge(k_st, 16 * t)
                dve.wait_ge(i_st, 16 * t)
                dve.wait_ge(ik_st, 16 * t)
                nc.vector.tensor_copy(KI[:, :, :].rearrange("p h n -> p (h n)"), psT[:, 0:11 * P]).then_inc(ki_ev, 1)
            own.end(NT, 4)

        @block.tensor
        def _(pe):
            pe.wait_ge(setup, 2)
            with pe.Fori(0, NT // 2) as t:
                for b in range(2):
                    n = 2 * t + b
                    pe.wait_ge(loaded[b], 16 * t + 16)
                    pe.wait_ge(ki_ev, n)
                    for k in range(9):
                        last = nc.tensor.transpose(psT[:, k * P:(k + 1) * P], a_t[:, b, k, :], ident[:, :])
                    last.then_inc(tok_ps, 1)
                    pe.wait_ge(lo_ok, n + 1)
                    pe.wait_ge(q_ev, n)
                    for h in range(AH):
                        for s in range(2):
                            at = (2 * h + s) * P
                            src = QHL[:, h, s, :, :].bitcast(F32)
                            last = nc.tensor.transpose(psQ[:, at:at + P], src, ident[:, :])
                    last.then_inc(q_ps, 1)
                    pe.wait_ge(ilo_ok, n + 1)
                    pe.wait_ge(tok_ok, n + 1)
                    for g in range(AKV):
                        nc.tensor.transpose(psT[:, g * P:(g + 1) * P], KHL[:, g, :, :].bitcast(F32), ident[:, :])
                    for h in range(IH + 1):
                        src = (IHL[:, h, :, :, :] if h < IH else IKL[:, :, :, :]).bitcast(F32)
                        last = nc.tensor.transpose(psT[:, (2 + h) * P:(3 + h) * P], src, ident[:, :])
                    last.then_inc(ki_ps, 1)


def sparse_attention(pg):
    nc = pg.nc
    y_d = pg.dram("y_attT", (P, AH // 2, SEQ))
    with ExitStack() as c:
        sb = lambda n, s, d=F32: c.enter_context(nc.sbuf_tensor(n, s, d))
        B = dict(
            IK=sb("ik_all", [P, SEQ], F32R), IQ=sb("iq_blk", [P, 2, IH, P], F32R), IW=sb("iw_all", [P, NT, IH]),
            KS=sb("k_all", [P, AKV, SEQ], F32R), QS=sb("q_blk", [P, 2, AH, 2, P], F32R), V=sb("v_all", [P, NT, AKV, P]),
            KEY=sb("key_index", [P, SEQ]), LIM=sb("key_limit", [P, NT]), lim=sb("block_limit", [P, 1]), A=sb("score", [P, 4, SEQ]), S=sb("score_signed", [P, 4, SEQ]),
            R=sb("relu", [P, 2, SEQ]), VB=sb("visible_bias", [P, 2, SEQ]), MB=sb("mask_bias", [P, 4, SEQ], BF16),
            BIT=sb("bits", [P, 32], I32), BITF=sb("bits_f", [P, 31]), idf=sb("ident4", [P, P]), idb=sb("ident4b", [P, P], BF16),
            ones=sb("ones_r", [P, P], F32R), onei=sb("one_i", [P, 4], I32),
            cnt=sb("count", [P, 4]), pos=sb("is_pos", [P, 4]), sg=sb("sign", [P, 4]), need=sb("need", [P, 4]), thr=sb("count_thr", [P, 4]),
            cand=sb("cand", [P, 4], I32), miss=sb("miss", [P, 4]), drop=sb("drop", [P, 4], I32), nxt=sb("next_up", [P, 4], I32),
            t=sb("kth", [P, 4]), ties=sb("ties", [P, 4]),
            mxp=sb("max_part", [P, AH, 2]), nmx=sb("neg_max", [P, AH]), D=sb("diag_max", [P, 2, 4, P], F32R),
            PT=sb("probT", [P, 2, 512]), RS=sb("inv_sum", [AD, 2, 512]), Y=sb("y_blk", [P, AH // 2, P]))
        attention_constants(pg, B)
        for g in range(NCH):
            with ExitStack() as s:
                select_keys(pg, B, g, s)
            with ExitStack() as s:
                attend(pg, B, g, s, y_d)


def attention_constants(pg, B):
    nc = pg.nc
    with ExitStack() as c:
        sem = pg.semaphores(c)
        ints = B["VB"][:, 0, :].bitcast(I32)
        lim = c.enter_context(nc.sbuf_tensor("c4_lim", [P, NT], I32))
        loads, idf, idb, idx = (sem("c4_" + n) for n in ("loads", "idf", "idb", "idx"))
        block = c.enter_context(nc.Block())

        @block.sync
        def _(sp):
            sp.dma_start(B["IK"][:, :].bitcast(F32), pg.d["ik_stack"]).then_inc(loads, 16)
            sp.dma_start(B["KS"][:, :, :].bitcast(F32), pg.d["k_stack"]).then_inc(loads, 16)
            sp.dma_start(B["V"][:, :, :, 0:AD], pg.d["v"]).then_inc(loads, 16)
            sp.dma_start(B["IW"][:, :, :], pg.d["iw"]).then_inc(loads, 16)
            sp.wait_ge(loads, 64)

        @block.gpsimd
        def _(pool):
            identity(nc, pool, B["idf"][:, :], idf)
            identity(nc, pool, B["idb"][:, :], idb)
            nc.gpsimd.memset(B["V"][:, :, :, AD:P], 1.0)
            nc.gpsimd.memset(B["onei"][:, :], 1)
            nc.gpsimd.memset(B["t"][:, :], 1.0)
            nc.gpsimd.iota(ints, [[1, SEQ]], base=0, channel_multiplier=0)
            nc.gpsimd.iota(lim[:, :], [[P, NT]], base=64, channel_multiplier=0)
            for n in range(31):
                nc.gpsimd.memset(B["BIT"][:, n:n + 1], 1 << (30 - n))
            nc.gpsimd.memset(B["BIT"][:, 31:32], 0).then_inc(idx, 1)

        @block.vector
        def _(dve):
            dve.wait_ge(idx, 1)
            nc.vector.tensor_copy(B["KEY"][:, :], ints)
            dve.wait_ge(loads, 64)
            nc.vector.tensor_scalar(B["IW"][:, :, :], B["IW"][:, :, :], (IH * ID) ** -0.5, None, ALU.mult)
            nc.vector.tensor_copy(B["LIM"][0:64, :], lim[0:64, :])
            nc.vector.tensor_scalar(B["LIM"][64:P, :], lim[64:P, :], 64.0, None, ALU.add)
            nc.vector.tensor_copy(B["BITF"][:, :], B["BIT"][:, 0:31])

        @block.scalar
        def _(act):
            act.wait_ge(idf, 2)
            nc.scalar.activation(B["ones"][:, :], B["idf"][:, :], ACT.Exp, scale=0.0)


def select_keys(pg, B, g, c):
    nc = pg.nc
    W = 512 * (g + 1)
    sem = pg.semaphores(c, f"g{g}_")
    ps = c.enter_context(nc.psum_tensor(f"z_{g}", [P, 2, SEQ], F32))
    gt, eq, cum = (B["R"][:, 0, 0:W], B["R"][:, 1, 0:W], B["VB"][:, 0, 0:W])
    iq_in = [sem(f"iq_in{b}") for b in range(2)]
    held = sem("held")
    vb_ok, z_ok, relu_ok, sum_ok, cand_ok, act_cnt, own = (sem(n) for n in ("vb_ok", "z_ok", "relu_ok", "sum_ok", "cand_ok", "act_cnt", "s_own"))
    A, S, R, VB = B["A"], B["S"], B["R"], B["VB"]
    unused = [R[:, j // 2, (j % 2) * 1024:(j % 2 + 1) * 1024].bitcast(BF16)[:, 0:W] for j in range(4)]
    block = c.enter_context(nc.Block())

    @block.sync
    def _(sp):
        with sp.Fori(0, 2) as t:
            for b in range(2):
                sp.wait_ge(z_ok, 16 * t)
                sp.dma_start(B["IQ"][:, b, :, :].bitcast(F32), pg.d["iq_stack"][bass.ds(4 * g + 2 * t + b, 1)]
                             .rearrange("o p (h n) -> (o p) h n", n=P)).then_inc(iq_in[b], 16)

    @block.gpsimd
    def _(pool):
        with pool.Fori(0, 2) as t:
            for b in range(2):
                pool.wait_ge(vb_ok, 2 * (2 * t + b))
                nc.gpsimd.tensor_copy(B["lim"][:, :], B["LIM"][:, bass.ds(4 * g + 2 * t + b, 1)]).then_inc(vb_ok, 1)
                pool.wait_ge(vb_ok, 2 * (2 * t + b) + 1)
                pool.wait_ge(sum_ok, 16 * t)
                hold(pool, held)
                nc.gpsimd.tensor_scalar(VB[:, b, 0:W], B["KEY"][:, 0:W], B["lim"][:, :], NEG, ALU.is_ge, ALU.mult).then_inc(vb_ok, 1)

    @block.tensor
    def _(pe):
        with pe.Fori(0, 2) as t:
            for b in range(2):
                pe.wait_ge(iq_in[b], 16 * t + 16)
                for h in range(IH):
                    pe.wait_ge(relu_ok, 16 * t + 8 * b + max(h - 1, 0))
                    for q in range(g + 1):
                        last = nc.tensor.matmul(ps[:, h % 2, q * 512:(q + 1) * 512], B["IQ"][:, b, h, :],
                                                B["IK"][:, q * 512:(q + 1) * 512], start=True, stop=True)
                    last.then_inc(z_ok, 1)

    @block.scalar
    def _(act):
        with act.Fori(0, 2) as t:
            for b in range(2):
                for h in range(IH):
                    n = 16 * t + 8 * b
                    act.wait_ge(z_ok, n + h + 1)
                    act.wait_ge(sum_ok, n + max(h - 1, 0))
                    nc.scalar.activation(R[:, h % 2, 0:W], ps[:, h % 2, 0:W], ACT.Relu).then_inc(relu_ok, 1)
        with act.Fori(0, 31) as n:
            act.wait_ge(cand_ok, n + 1)
            for j in (2, 3):
                last = nc.scalar.activation(unused[j], S[:, j, 0:W], ACT.Sign, bias=B["cand"][:, j:j + 1].bitcast(F32),
                                            accum_out=B["cnt"][:, j:j + 1])
                last.then_inc(act_cnt, 1)

    @block.vector
    def _(dve):
        own_ = Steps(dve, own)
        with dve.Fori(0, 2) as t:
            for b in range(2):
                j = 2 * t + b
                acc = A[:, bass.ds(j, 1), 0:W].rearrange("p o n -> p (o n)")
                dve.wait_ge(vb_ok, 2 * (2 * t + b) + 2)
                for h in range(IH):
                    n = 16 * t + 8 * b + h
                    dve.wait_ge(relu_ok, n + 1)
                    dve.wait_ge(sum_ok, n)
                    nc.vector.scalar_tensor_tensor(out=acc, in0=R[:, h % 2, 0:W], scalar=B["IW"][:, bass.ds(4 * g + j, 1), h],
                                                   in1=VB[:, b, 0:W] if h == 0 else acc, op0=ALU.mult, op1=ALU.add).then_inc(sum_ok, 1)
        dve.wait_ge(sum_ok, 32)
        cnt, pos, sg, need, thr = (B[n][:, :] for n in ("cnt", "pos", "sg", "need", "thr"))
        cand, miss, drop, nxt = (B[n][:, :] for n in ("cand", "miss", "drop", "nxt"))
        for j in range(4):
            last = nc.vector.tensor_scalar(S[:, j, 0:W], A[:, j, 0:W], 0.0, 0.0, ALU.is_ge, ALU.add, accum_out=B["cnt"][:, j:j + 1])
        own_(last)
        own_(nc.vector.tensor_scalar(pos, cnt, float(TOPK), None, ALU.is_ge))
        nc.vector.tensor_scalar(sg, pos, 2.0, -1.0, ALU.mult, ALU.add)
        own_(nc.vector.tensor_scalar(need, pos, float(2 * TOPK - 1 - W), float(W - TOPK + 1), ALU.mult, ALU.add))
        nc.vector.tensor_copy(B["thr"][:, 0:2], B["need"][:, 0:2])
        own_(nc.vector.tensor_scalar(B["thr"][:, 2:4], B["need"][:, 2:4], 2.0, float(-W), ALU.mult, ALU.add))
        for j in range(4):
            nc.vector.tensor_scalar(S[:, j, 0:W], A[:, j, 0:W], B["sg"][:, j:j + 1], None, ALU.mult)
        nc.vector.memset(B["cand"][:, 0:2], 1 << 30)
        nc.vector.memset(B["cand"][:, 2:4].bitcast(F32), -2.0).then_inc(cand_ok, 1)
        dve.wait_ge(cand_ok, 1)
        own_.end(1, own_.k)
        with dve.Fori(0, 31) as n:
            own_.body(n * 3)
            for j in (0, 1):
                last = nc.vector.tensor_scalar(unused[j], S[:, j, 0:W], B["cand"][:, j:j + 1].bitcast(F32), 0.0, ALU.is_ge, ALU.add,
                                               accum_out=B["cnt"][:, j:j + 1])
            own_(last)
            dve.wait_ge(act_cnt, 2 * n + 2)
            own_(nc.vector.tensor_tensor(miss, cnt, thr, ALU.is_lt))
            own_(nc.vector.tensor_tensor(drop, miss, B["BITF"][:, bass.ds(n, 1)].broadcast_to([P, 4]), ALU.mult))
            nc.vector.scalar_tensor_tensor(out=cand, in0=drop, scalar=B["BIT"][:, bass.ds(n + 1, 1)], in1=cand,
                                           op0=ALU.bitwise_xor, op1=ALU.bitwise_xor).then_inc(cand_ok, 1)
            dve.wait_ge(cand_ok, n + 2)
        own_.end(31, 3)
        own_(nc.vector.tensor_scalar(B["cand"][:, 2:4].bitcast(F32), B["cand"][:, 2:4].bitcast(F32), -1.0, None, ALU.mult))
        own_(nc.vector.tensor_tensor(nxt, cand, B["onei"][:, :], ALU.add))
        for j in (2, 3):
            last = nc.vector.tensor_scalar(unused[j], S[:, j, 0:W], B["nxt"][:, j:j + 1].bitcast(F32), 0.0, ALU.is_ge, ALU.add,
                                           accum_out=B["cnt"][:, j:j + 1])
        own_(last)
        own_(nc.vector.tensor_tensor(B["drop"][:, 2:4], B["cnt"][:, 2:4], B["need"][:, 2:4], ALU.is_ge))
        own_(nc.vector.tensor_tensor(B["cand"][:, 2:4], B["cand"][:, 2:4], B["drop"][:, 2:4], ALU.add))
        own_(nc.vector.tensor_tensor(B["t"][:, :], cand.bitcast(F32), sg, ALU.mult))
        for j in range(4):
            own_(nc.vector.tensor_scalar(gt, A[:, j, 0:W], B["t"][:, j:j + 1], 0.0, ALU.is_gt, ALU.add, accum_out=B["cnt"][:, j:j + 1]))
            nc.vector.tensor_scalar(B["ties"][:, j:j + 1], B["cnt"][:, j:j + 1], -1.0, float(TOPK), ALU.mult, ALU.add)
            own_(nc.vector.tensor_scalar(eq, A[:, j, 0:W], B["t"][:, j:j + 1], None, ALU.is_equal))
            own_(nc.vector.tensor_tensor_scan(cum, eq, eq, 0.0, ALU.add, ALU.bypass))
            own_(nc.vector.scalar_tensor_tensor(out=cum, in0=cum, scalar=B["ties"][:, j:j + 1], in1=eq, op0=ALU.is_le, op1=ALU.mult))
            own_(nc.vector.tensor_tensor(gt, gt, cum, ALU.add))
            if g == 0:
                own_(nc.vector.scalar_tensor_tensor(out=gt, in0=B["KEY"][:, 0:W], scalar=B["LIM"][:, j:j + 1], in1=gt,
                                                    op0=ALU.is_lt, op1=ALU.mult))
            own_(nc.vector.tensor_scalar(B["MB"][:, j, 0:W], gt, -1.0, -NEG, ALU.add, ALU.mult))


def attend(pg, B, g, c, y_d):
    nc = pg.nc
    W = 512 * (g + 1)
    J = W // P
    PW = min(W, 1024)
    NPC = -(-W // PW)
    sem = pg.semaphores(c, f"g{g}_")
    L = c.enter_context(nc.psum_tensor(f"logits_{g}", [P, 2, 1024], F32))
    ST = c.enter_context(nc.psum_tensor(f"logitsT_{g}", [P, 2, 512], F32))
    O = c.enter_context(nc.psum_tensor(f"attn_{g}", [P, AKV, 512], F32))
    q_in = [sem(f"q_in{b}") for b in range(2)]
    held = sem("t_held")
    l_ok, mx_ok, nm_ok, d_ok, st_ok, p_ok, pv_ok, rs_ok, y_ok, y_st = (sem("t_" + n) for n in (
        "l_ok", "mx_ok", "nm_ok", "d_ok", "st_ok", "p_ok", "pv_ok", "rs_ok", "y_ok", "y_st"))
    QS, KS, V, MB, D, PT, RS, Y = (B[n] for n in ("QS", "KS", "V", "MB", "D", "PT", "RS", "Y"))
    R4 = AH // AKV
    LB = AH * NPC
    block = c.enter_context(nc.Block())

    def pieces(h):
        return [(p, p * PW, min(W, (p + 1) * PW)) for p in range(NPC)]

    @block.sync
    def _(sp):
        with sp.Fori(0, 2) as t:
            for b in range(2):
                sp.wait_ge(pv_ok, 4 * J * t)
                sp.dma_start(QS[:, b, :, :, :].bitcast(F32), pg.d["q_stack"][bass.ds(4 * g + 2 * t + b, 1)]
                             .rearrange("o p (h s n) -> (o p) h s n", s=2, n=P)).then_inc(q_in[b], 16)
            for b in range(2):
                n = 2 * t + b
                sp.wait_ge(y_ok, 2 * n + 2)
                sp.dma_start(y_d[:, :, bass.ds((4 * g + n) * P, P)], Y[:, :, :]).then_inc(y_st, 16)
        sp.wait_ge(y_st, 64)

    @block.tensor
    def _(pe):
        with pe.Fori(0, 2) as t:
            for b in range(2):
                n = 2 * t + b
                pe.wait_ge(q_in[b], 16 * t + 16)
                k = 0
                for h in range(AH):
                    for p, lo, hi in pieces(h):
                        pe.wait_ge(mx_ok, n * LB + max(k - 1, 0))
                        for a in range(lo, hi, 512):
                            o = L[:, k % 2, a - lo:a - lo + 512]
                            nc.tensor.matmul(o, QS[:, b, h, 0, :], KS[:, h // R4, a:a + 512], start=True, stop=False)
                            nc.tensor.matmul(o, QS[:, b, h, 1, :], KS[:, h // R4, a:a + 512], start=False, stop=False)
                            last = nc.tensor.matmul(o, B["idb"][:, :], MB[:, bass.ds(n, 1), a:a + 512].rearrange("p o n -> p (o n)"),
                                                    start=False, stop=True)
                        last.then_inc(l_ok, 1)
                        k += 1
                for v in range(AKV):
                    u0 = (2 * n + v) * J
                    pe.wait_ge(d_ok, 2 * n + v + 1)

                    def pv(j):
                        pe.wait_ge(p_ok, u0 + j + 1)
                        last = nc.tensor.matmul(O[:, v, :], V[:, j, v, :], PT[:, j % 2, :], start=(j == 0), stop=(j == J - 1))
                        last.then_inc(pv_ok, 1)
                    for j in range(J):
                        pe.wait_ge(p_ok, u0 + max(j - 1, 0))
                        o = ST[:, j % 2, :]
                        kj = KS[:, v, j * P:(j + 1) * P]
                        for s in range(2):
                            nc.tensor.matmul(o, kj, QS[:, b, v * R4:(v + 1) * R4, s, :], start=(s == 0), stop=False)
                        nc.tensor.matmul(o, B["ones"][:, :], D[:, v, :, :].rearrange("p h n -> p (h n)"), start=False, stop=False)
                        nc.tensor.matmul(o, MB[:, bass.ds(n, 1), j * P:(j + 1) * P].rearrange("p o n -> p (o n)"),
                                         B["idb"][:, :].unsqueeze(1).broadcast_to([P, R4, P]), start=False, stop=True).then_inc(st_ok, 1)
                        if j == 0:
                            pe.wait_ge(y_ok, 2 * n)
                        else:
                            pv(j - 1)
                    pv(J - 1)

    @block.scalar
    def _(act):
        with act.Fori(0, 2) as t:
            for b in range(2):
                n = 2 * t + b
                for v in range(AKV):
                    u0 = (2 * n + v) * J
                    for j in range(J):
                        act.wait_ge(st_ok, u0 + j + 1)
                        act.wait_ge(pv_ok, u0 + max(j - 1, 0))
                        nc.scalar.activation(PT[:, j % 2, :], ST[:, j % 2, :], ACT.Exp).then_inc(p_ok, 1)

    @block.gpsimd
    def _(pool):
        with pool.Fori(0, 4) as n:
            for v in range(AKV):
                pool.wait_ge(nm_ok, 2 * n + v + 1)
                hold(pool, held)
                for h in range(R4):
                    last = nc.gpsimd.tensor_scalar(D[:, v, h, :], B["idf"][:, :], B["nmx"][:, v * R4 + h:v * R4 + h + 1], None, ALU.mult)
                last.then_inc(d_ok, 1)

    @block.vector
    def _(dve):
        with dve.Fori(0, 4) as n:
            k = 0
            for v in range(AKV):
                for h in range(v * R4, (v + 1) * R4):
                    for p, lo, hi in pieces(h):
                        dve.wait_ge(l_ok, n * LB + k + 1)
                        nc.vector.reduce_max(B["mxp"][:, h, p:p + 1], L[:, k % 2, 0:hi - lo], AX.X).then_inc(mx_ok, 1)
                        k += 1
                dve.wait_ge(mx_ok, n * LB + k)
                dve.wait_ge(st_ok, 2 * n * J)
                nc.vector.tensor_reduce(B["nmx"][:, v * R4:(v + 1) * R4], B["mxp"][:, v * R4:(v + 1) * R4, 0:NPC], AX.X, ALU.max,
                                        negate=True).then_inc(nm_ok, 1)
            for v in range(AKV):
                dve.wait_ge(pv_ok, (2 * n + v + 1) * J)
                nc.vector.reciprocal(RS[:, v, :], O[AD:P, v, :]).then_inc(rs_ok, 1)
                dve.wait_ge(rs_ok, 2 * n + v + 1)
                dve.wait_ge(y_st, 16 * n)
                rs = RS[:, v, :].rearrange("p (m s n) -> p m s n", s=2, n=P)
                ov = O[0:AD, v, :].rearrange("p (m s n) -> p m s n", s=2, n=P)
                for s in range(2):
                    last = nc.vector.tensor_tensor(Y[s * AD:(s + 1) * AD, 2 * v:2 * v + 2, :], ov[:, :, s, :], rs[:, :, s, :], ALU.mult)
                last.then_inc(y_ok, 1)


def mlstm_gates(pg):
    nc, i = pg.nc, pg.i
    R = MH * NT
    m_d = pg.dram("m_neg_rows", (R, P))
    dec_d = pg.dram("decay_rows", (1, R))
    col_d = pg.dram("gate_cols", (P, 4, R))
    end_d, car_d = pg.dram("chunk_ends", (R, 2)), pg.dram("chunk_carry", (R, 2))
    with ExitStack() as c:
        sb = lambda n, s, d=F32: c.enter_context(nc.sbuf_tensor(n, s, d))
        sem = pg.semaphores(c, "g_")
        F, I, e, l, b, d, cm, M = (sb("g_" + n, [R, P]) for n in ("F", "I", "e", "l", "b", "d", "cm", "M"))
        W = sb("g_W", [R, 4, P])
        bi, bf, one = (sb("g_" + n, [R, 1]) for n in ("bi", "bf", "one"))
        ends, car, x1, x2 = sb("g_ends", [R, 2]), sb("g_car", [R, 2]), sb("g_x1", [R, 1]), sb("g_x2", [R, 1])
        dec = sb("g_dec", [R, 1])
        E4, C4 = sb("g_E4", [MH, NT, 2]), sb("g_C4", [MH, NT + 1])
        C2 = sb("g_C2", [MH, NT, 2])
        cols = sb("g_cols", [P, 4, R])
        ident = sb("g_ident", [P, P])
        ps = c.enter_context(nc.psum_tensor("g_ps", [P, 4, R], F32))
        loads, setup, own, ex, dma, w_ok, tr, ev = (sem(n) for n in ("loads", "setup", "own", "ex", "dma", "w_ok", "tr", "ev"))
        block = c.enter_context(nc.Block())

        @block.gpsimd
        def _(pool):
            identity(nc, pool, ident[:, :], setup)
            nc.gpsimd.memset(one[:, :], 1.0).then_inc(setup, 1)
            nc.gpsimd.memset(C4[:, 0:1], 0.0).then_inc(setup, 1)

        @block.sync
        def _(sp):
            rows = lambda at: pg.d["projT"][at:at + MH, :].rearrange("h (c n) -> (h c) n", n=P)
            sp.dma_start(I[:, :], rows(C_IF)).then_inc(loads, 16)
            sp.dma_start(F[:, :], rows(C_IF + MH)).then_inc(loads, 16)
            sp.dma_start(bi[:, :], i["b_igate"]).then_inc(loads, 16)
            sp.dma_start(bf[:, :], i["b_fgate"]).then_inc(loads, 16)
            sp.wait_ge(w_ok, 1)
            sp.dma_start(end_d, ends[:, :]).then_inc(dma, 16)
            sp.wait_ge(dma, 16)
            sp.dma_start(E4[:, :, :], end_d.rearrange("(h c) k -> h c k", c=NT)).then_inc(dma, 16)
            sp.wait_ge(w_ok, 2)
            sp.dma_start(car_d.rearrange("(h c) k -> h c k", c=NT), C2[:, :, :]).then_inc(dma, 16)
            sp.wait_ge(dma, 48)
            sp.dma_start(car[:, :], car_d).then_inc(dma, 16)
            sp.wait_ge(w_ok, 3)
            sp.wait_ge(ex, 6)
            sp.wait_ge(ev, 1)
            sp.dma_start(m_d, M[:, :]).then_inc(dma, 16)
            sp.dma_start(dec_d.rearrange("o r -> r o"), dec[:, :]).then_inc(dma, 16)
            sp.dma_start(col_d, cols[:, :, :]).then_inc(dma, 16)
            sp.wait_ge(dma, 112)

        @block.scalar
        def _(act):
            act.wait_ge(setup, 4)
            act.wait_ge(own, 2)
            nc.scalar.activation(e[:, :], l[:, :], ACT.Exp, scale=-1.0).then_inc(ex, 1)
            act.wait_ge(ex, 1)
            nc.scalar.activation(l[:, :], e[:, :], ACT.Ln, bias=one[:, :]).then_inc(ex, 1)
            act.wait_ge(w_ok, 3)
            nc.scalar.activation(W[:, 1, :], W[:, 1, :], ACT.Exp).then_inc(ex, 1)
            nc.scalar.activation(W[:, 2, :], W[:, 2, :], ACT.Exp).then_inc(ex, 1)
            nc.scalar.activation(W[:, 3, :], W[:, 3, :], ACT.Exp).then_inc(ex, 1)
            nc.scalar.activation(dec[:, :], dec[:, :], ACT.Exp).then_inc(ex, 1)

        @block.vector
        def _(dve):
            s = Steps(dve, own)
            v = nc.vector
            dve.wait_ge(loads, 64)
            s(v.tensor_scalar(F[:, :], F[:, :], bf[:, :], None, ALU.add))
            s(v.scalar_tensor_tensor(out=l[:, :], in0=F[:, :], scalar=-1.0, in1=F[:, :], op0=ALU.mult, op1=ALU.max))
            v.tensor_scalar(F[:, :], F[:, :], 0.0, None, ALU.min)
            s(v.tensor_scalar(I[:, :], I[:, :], bi[:, :], None, ALU.add))
            dve.wait_ge(ex, 2)
            s(v.tensor_tensor(F[:, :], F[:, :], l[:, :], ALU.subtract))
            s(v.tensor_tensor_scan(b[:, :], F[:, :], F[:, :], 0.0, ALU.add, ALU.bypass))
            s(v.tensor_tensor(d[:, :], I[:, :], b[:, :], ALU.subtract))
            s(v.tensor_tensor_scan(cm[:, :], d[:, :], d[:, :], -3e38, ALU.max, ALU.bypass))
            v.tensor_copy(ends[:, 0:1], b[:, P - 1:P])
            v.tensor_tensor(ends[:, 1:2], b[:, P - 1:P], cm[:, P - 1:P], ALU.add).then_inc(w_ok, 1)
            dve.wait_ge(dma, 32)
            dve.wait_ge(setup, 4)
            s(v.tensor_tensor_scan(C4[:, 1:NT + 1], E4[:, :, 0], E4[:, :, 1], 0.0, ALU.add, ALU.max))
            v.tensor_copy(C2[:, :, 0], C4[:, 0:NT])
            v.tensor_copy(C2[:, :, 1], C4[:, 1:NT + 1]).then_inc(w_ok, 1)
            dve.wait_ge(dma, 64)
            s(v.tensor_scalar(M[:, :], cm[:, :], car[:, 0:1], None, ALU.max))
            s(v.tensor_tensor(x1[:, :], ends[:, 0:1], car[:, 1:2], ALU.subtract))
            v.tensor_tensor(dec[:, :], x1[:, :], car[:, 0:1], ALU.add)
            v.tensor_scalar(W[:, 3, :], d[:, :], x1[:, :], None, ALU.add)
            v.tensor_scalar(W[:, 1, :], M[:, :], -1.0, car[:, 0:1], ALU.mult, ALU.add)
            s(v.tensor_tensor(W[:, 2, :], b[:, :], M[:, :], ALU.add))
            v.tensor_scalar(W[:, 2, :], W[:, 2, :], -1.0, None, ALU.mult)
            v.tensor_copy(W[:, 0, :], d[:, :])
            v.tensor_scalar(M[:, :], M[:, :], -1.0, None, ALU.mult).then_inc(w_ok, 1)
            dve.wait_ge(tr, 1)
            v.tensor_copy(cols[:, :, :], ps[:, :, :]).then_inc(ev, 1)

        @block.tensor
        def _(pe):
            pe.wait_ge(setup, 2)
            pe.wait_ge(w_ok, 3)
            pe.wait_ge(ex, 6)
            for k in range(4):
                last = nc.tensor.transpose(ps[:, k, :], W[:, k, :], ident[0:R, 0:R])
            last.then_inc(tr, 1)


def mlstm_conv(pg):
    nc, i = pg.nc, pg.i
    qk_d = pg.dram("qkT", (2 * MH, P, SEQ))
    H = CONV - 1
    with ExitStack() as c:
        sb = lambda n, s, d=F32: c.enter_context(nc.sbuf_tensor(n, s, d))
        sem = pg.semaphores(c, "v_")
        U, Y, G = (sb("v_" + n, [P, 2, s]) for n, s in (("U", H + SEQ), ("Y", SEQ), ("G", SEQ)))
        ks = sb("v_scale", [P, 2 * MH])
        wt, bt = sb("v_w", [P, CONV, 2 * MH]), sb("v_b", [P, 2 * MH])
        u_in = [sem(f"u{b}") for b in range(2)]
        st = [pg.sw_sem(f"conv_stored{b}") for b in range(2)]
        consts, pad, y0, y_ok, g_ok, o_ok = (sem(n) for n in ("consts", "pad", "y0", "y_ok", "g_ok", "o_ok"))
        block = c.enter_context(nc.Block())

        @block.sync
        def _(sp):
            sp.dma_start(wt[:, :, :], i["w_conv_mlstm"]).then_inc(consts, 16)
            sp.dma_start(bt[:, :], i["b_conv_mlstm"]).then_inc(consts, 16)
            with sp.Fori(0, MH) as t:
                for b in range(2):
                    sp.wait_ge(y_ok, 2 * t)
                    sp.dma_start(U[:, b, H:H + SEQ], pg.d["projT"][bass.ds(C_MQK + (2 * t + b) * P, P), :]).then_inc(u_in[b], 16)

        @block.gpsimd
        def _(pool):
            nc.gpsimd.memset(ks[:, 0:MH], 1.0)
            nc.gpsimd.memset(ks[:, MH:2 * MH], MD ** -0.5)
            nc.gpsimd.memset(U[:, :, 0:H], 0.0).then_inc(pad, 1)
            with pool.Fori(0, MH) as t:
                for b in range(2):
                    pool.wait_ge(o_ok, 2 * t + b + 1)
                    pool.dma_start(qk_d[bass.ds(2 * t + b, 1)].rearrange("o p n -> (o p) n"), G[:, b, :]).then_inc(st[b], 16)
            for b in range(2):
                pool.wait_ge(st[b], 16 * MH)

        @block.scalar
        def _(act):
            act.wait_ge(consts, 32)
            act.wait_ge(pad, 1)
            with act.Fori(0, MH) as t:
                for b in range(2):
                    act.wait_ge(u_in[b], 16 * t + 16)
                    act.wait_ge(o_ok, 2 * t)
                    nc.scalar.activation(Y[:, b, :], U[:, b, 0:SEQ], ACT.Identity, scale=wt[:, 0, bass.ds(2 * t + b, 1)],
                                         bias=bt[:, bass.ds(2 * t + b, 1)]).then_inc(y0, 1)
                for b in range(2):
                    act.wait_ge(y_ok, 2 * t + b + 1)
                    act.wait_ge(st[b], 16 * t)
                    nc.scalar.activation(G[:, b, :], Y[:, b, :], ACT.Sigmoid).then_inc(g_ok, 1)

        @block.vector
        def _(dve):
            own = Steps(dve, sem("own"))
            dve.wait_ge(pad, 1)
            with dve.Fori(0, MH) as t:
                own.body(t * 2 * (CONV - 2))
                for b in range(2):
                    dve.wait_ge(y0, 2 * t + b + 1)
                    for j in range(1, CONV):
                        last = nc.vector.scalar_tensor_tensor(out=Y[:, b, :], in0=U[:, b, j:j + SEQ], scalar=wt[:, j, bass.ds(2 * t + b, 1)],
                                                              in1=Y[:, b, :], op0=ALU.mult, op1=ALU.add)
                        if j < CONV - 1:
                            own(last)
                    last.then_inc(y_ok, 1)
                for b in range(2):
                    dve.wait_ge(g_ok, 2 * t + b + 1)
                    nc.vector.scalar_tensor_tensor(out=G[:, b, :], in0=G[:, b, :], scalar=ks[:, bass.ds(2 * t + b, 1)],
                                                   in1=Y[:, b, :], op0=ALU.mult, op1=ALU.mult).then_inc(o_ok, 1)
            own.end(MH, 2 * (CONV - 2))


def mlstm_scan(pg):
    nc, i = pg.nc, pg.i
    y_d = pg.dram("y_mlT", (P, MH, SEQ))
    E1 = MD + 1
    with ExitStack() as c:
        sb = lambda n, s, d=F32: c.enter_context(nc.sbuf_tensor(n, s, d))
        sem = pg.semaphores(c, "m_")
        X = sb("m_X", [P, 2, 4, MH, P])
        COL = sb("m_COL", [P, 4, MH, NT])
        MN, DEC = sb("m_MN", [P, MH, NT, P]), sb("m_DEC", [P, MH, NT])
        CAUS, IDN = sb("m_caus", [P, P]), sb("m_ident", [P, P])
        AR, PT, KW, T1, T2, SQ, SG = (sb("m_" + n, [P, MH, P]) for n in ("AR", "PT", "KW", "T1", "T2", "SQ", "SG"))
        VO, CN, N1 = (sb("m_" + n, [P, MH, E1]) for n in ("VO", "CN", "N1"))
        GN = sb("m_gain", [P, MH, MD])
        YM = sb("m_Y", [P, 2, MH, P])
        den, rec, ss, ms, rt, rs, sc = (sb("m_" + n, [P, MH]) for n in ("den", "rec", "ss", "ms", "rt", "rs", "sc"))
        eps = sb("m_eps", [P, 1])
        pt = lambda n, s: c.enter_context(nc.psum_tensor("m_" + n, s, F32))
        psS, psI, psO, psU = pt("pS", [P, MH, P]), pt("pI", [P, 2, 2, 256]), pt("pO", [P, 2, 2, 256]), pt("pU", [P, 1024])
        psY = pt("pY", [P, MH, P])
        hv = lambda z: z.rearrange("p (a b) n -> p a b n", b=2)
        uE = psU[:, :].rearrange("p (a b n) -> p a b n", a=2, b=2)
        x_in = [sem(f"x{b}") for b in range(2)]
        st = [pg.sw_sem(f"scan_stored{b}") for b in range(2)]
        (consts, setup, ar_ok, e_ok, s_ps, kv_ps, i_ps, o_ps, u_ps, pt_ok, kw_ok, v_ok, cn_ok, num_ok, abs_ok, sq_ok, ms_ok, rt_ok,
         h_ok, y_ps, sg_ok, ym_ok) = (sem(n) for n in (
            "consts", "setup", "ar_ok", "e_ok", "s_ps", "kv_ps", "i_ps", "o_ps", "u_ps", "pt_ok", "kw_ok", "v_ok", "cn_ok", "num_ok",
            "abs_ok", "sq_ok", "ms_ok", "rt_ok", "h_ok", "y_ps", "sg_ok", "ym_ok"))
        own = sem("own")
        block = c.enter_context(nc.Block())

        @block.sync
        def _(sp):
            sp.dma_start(COL[:, :, :, :], pg.d["gate_cols"].rearrange("p k (h c) -> p k h c", c=NT)).then_inc(consts, 16)
            sp.dma_start(MN[:, :, :, :].rearrange("p h c n -> p (h c n)"), pg.d["m_neg_rows"].rearrange("r n -> (r n)").partition_broadcast(P)
                         ).then_inc(consts, 16)
            sp.dma_start(DEC[:, :, :].rearrange("p h c -> p (h c)"), pg.d["decay_rows"][0].partition_broadcast(P)).then_inc(consts, 16)
            sp.dma_start(GN[:, :, :].rearrange("p h n -> p (h n)"), i["g_norm_mlstm_out"].partition_broadcast(P)).then_inc(consts, 16)
            with sp.Fori(0, NT // 2) as t:
                for b in range(2):
                    sp.wait_ge(ym_ok, 2 * t)
                    at = bass.ds((2 * t + b) * P, P)
                    for k in range(2):
                        sp.dma_start(X[:, b, k, :, :], pg.d["qkT"][k * MH:(k + 1) * MH, :, at].rearrange("h p n -> p h n")).then_inc(x_in[b], 16)
                    for k, row in ((2, C_MV), (3, C_MO)):
                        sp.dma_start(X[:, b, k, :, :], pg.d["projT"][row:row + MH * MD, at].rearrange("(h p) n -> p h n", p=P)
                                     ).then_inc(x_in[b], 16)

        @block.gpsimd
        def _(pool):
            identity(nc, pool, IDN[:, :], setup)
            nc.gpsimd.memset(CN[:, :, :], 0.0)
            nc.gpsimd.memset(eps[:, :], EPS)
            nc.gpsimd.memset(VO[:, :, MD:E1], 1.0)
            nc.gpsimd.memset(CAUS[:, :], 0.0).then_inc(setup, 1)
            pool.wait_ge(setup, 3)
            nc.gpsimd.affine_select(out=CAUS[:, :], in_=CAUS[:, :], compare_op=ALU.is_ge, fill=NEG, base=0,
                                    pattern=[[1, P]], channel_multiplier=-1).then_inc(setup, 1)
            with pool.Fori(0, NT // 2) as t:
                for b in range(2):
                    pool.wait_ge(ym_ok, 2 * t + b + 1)
                    pool.dma_start(y_d[:, :, bass.ds((2 * t + b) * P, P)], YM[:, b, :, :]).then_inc(st[b], 16)
            for b in range(2):
                pool.wait_ge(st[b], 16 * (NT // 2))

        @block.tensor
        def _(pe):
            pe.wait_ge(setup, 4)
            with pe.Fori(0, NT // 2) as t:
                for b in range(2):
                    n = 2 * t + b
                    q, k, v = X[:, b, 0], X[:, b, 1], X[:, b, 2]
                    pe.wait_ge(x_in[b], 64 * t + 64)
                    pe.wait_ge(pt_ok, n)
                    for h in range(MH):
                        last = nc.tensor.matmul(psS[:, h, :], k[:, h, :], q[:, h, :], start=True, stop=True)
                    last.then_inc(s_ps, 1)
                    pe.wait_ge(cn_ok, n)
                    for h in range(MH):
                        nc.tensor.transpose(psU[:, h * P:(h + 1) * P], k[:, h, :], IDN[:, :])
                        last = nc.tensor.transpose(psU[:, 512 + h * P:512 + (h + 1) * P], v[:, h, :], IDN[:, :])
                    last.then_inc(kv_ps, 1)
                    for h in range(MH):
                        last = nc.tensor.matmul(psI[:, h // 2, h % 2, 0:E1], q[:, h, :], CN[:, h, :], start=True, stop=True)
                    last.then_inc(i_ps, 1)
                    pe.wait_ge(pt_ok, n + 1)
                    pe.wait_ge(v_ok, n + 1)
                    for h in range(MH):
                        last = nc.tensor.matmul(psO[:, h // 2, h % 2, 0:E1], PT[:, h, :], VO[:, h, :], start=True, stop=True)
                    last.then_inc(o_ps, 1)
                    pe.wait_ge(kw_ok, n + 1)
                    for h in range(MH):
                        last = nc.tensor.matmul(psU[:, h * 256:h * 256 + E1], KW[:, h, :], VO[:, h, :], start=True, stop=True)
                    last.then_inc(u_ps, 1)
                    pe.wait_ge(h_ok, n + 1)
                    for h in range(MH):
                        last = nc.tensor.transpose(psY[:, h, :], T2[:, h, :], IDN[:, :])
                    last.then_inc(y_ps, 1)

        @block.scalar
        def _(act):
            act.wait_ge(consts, 64)
            act.wait_ge(setup, 4)
            with act.Fori(0, NT // 2) as t:
                for b in range(2):
                    n = 2 * t + b
                    act.wait_ge(ar_ok, n + 1)
                    nc.scalar.activation(AR[:, :, :], AR[:, :, :], ACT.Exp).then_inc(e_ok, 1)
                    act.wait_ge(kv_ps, n + 1)
                    act.wait_ge(u_ps, n)
                    nc.scalar.copy(VO[:, :, 0:MD], psU[:, 512:1024].rearrange("p (h n) -> p h n", n=P)).then_inc(v_ok, 1)
                    act.wait_ge(num_ok, n + 1)
                    nc.scalar.activation(den[:, :], N1[:, :, MD], ACT.Abs).then_inc(abs_ok, 1)
                    nc.scalar.activation(SQ[:, :, :], N1[:, :, 0:MD], ACT.Square).then_inc(sq_ok, 1)
                    act.wait_ge(ms_ok, n + 1)
                    nc.scalar.activation(rt[:, :], ms[:, :], ACT.Sqrt, bias=eps[:, :], scale=1.0 / MD).then_inc(rt_ok, 1)
                    act.wait_ge(ym_ok, n)
                    nc.scalar.activation(SG[:, :, :], X[:, b, 3, :, :], ACT.Sigmoid).then_inc(sg_ok, 1)

        @block.vector
        def _(dve):
            v = nc.vector
            s = Steps(dve, own)
            bc = lambda z, w: z.broadcast_to([P, MH, w])
            dve.wait_ge(consts, 64)
            dve.wait_ge(setup, 4)
            with dve.Fori(0, NT // 2) as t:
                s.body(t * 18)
                for b in range(2):
                    n = 2 * t + b
                    at = bass.ds(n, 1)
                    col = lambda k: COL[:, k, :, at]
                    for h in range(MH):
                        last = v.scalar_tensor_tensor(out=AR[:, h, :], in0=MN[:, h, at, :].rearrange("p o n -> p (o n)"), scalar=COL[:, 0, h, at],
                                                      in1=CAUS[:, :], op0=ALU.add, op1=ALU.add)
                    last.then_inc(ar_ok, 1)
                    dve.wait_ge(kv_ps, n + 1)
                    v.tensor_tensor(KW[:, :, :], psU[:, 0:512].rearrange("p (h n) -> p h n", n=P), bc(col(3), P), ALU.mult).then_inc(kw_ok, 1)
                    dve.wait_ge(e_ok, n + 1)
                    dve.wait_ge(s_ps, n + 1)
                    v.tensor_tensor(PT[:, :, :], psS[:, :, :], AR[:, :, :], ALU.mult).then_inc(pt_ok, 1)
                    dve.wait_ge(i_ps, n + 1)
                    s(v.tensor_tensor(hv(N1[:, :, :]), psI[:, :, :, 0:E1], hv(COL[:, 1, :, at]).broadcast_to([P, 2, 2, E1]), ALU.mult))
                    s(v.tensor_tensor(CN[:, :, :], CN[:, :, :], bc(DEC[:, :, at], E1), ALU.mult))
                    dve.wait_ge(o_ps, n + 1)
                    v.tensor_tensor(hv(N1[:, :, :]), hv(N1[:, :, :]), psO[:, :, :, 0:E1], ALU.add).then_inc(num_ok, 1)
                    dve.wait_ge(u_ps, n + 1)
                    v.tensor_tensor(hv(CN[:, :, :]), hv(CN[:, :, :]), uE[:, :, :, 0:E1], ALU.add).then_inc(cn_ok, 1)
                    dve.wait_ge(abs_ok, n + 1)
                    s(v.tensor_tensor(den[:, :], den[:, :], COL[:, 2, :, at].rearrange("p h o -> p (h o)"), ALU.max))
                    s(v.reciprocal(rec[:, :], den[:, :]))
                    dve.wait_ge(sq_ok, n + 1)
                    s(v.tensor_reduce(ss[:, :], SQ[:, :, :], AX.X, ALU.add))
                    s(v.tensor_tensor(ms[:, :], ss[:, :], rec[:, :], ALU.mult))
                    v.tensor_tensor(ms[:, :], ms[:, :], rec[:, :], ALU.mult).then_inc(ms_ok, 1)
                    dve.wait_ge(rt_ok, n + 1)
                    s(v.reciprocal(rs[:, :], rt[:, :]))
                    s(v.tensor_tensor(sc[:, :], rec[:, :], rs[:, :], ALU.mult))
                    s(v.tensor_tensor(T1[:, :, :], N1[:, :, 0:MD], bc(sc[:, :].unsqueeze(2), MD), ALU.mult))
                    v.tensor_tensor(T2[:, :, :], T1[:, :, :], GN[:, :, :], ALU.mult).then_inc(h_ok, 1)
                    dve.wait_ge(y_ps, n + 1)
                    dve.wait_ge(sg_ok, n + 1)
                    dve.wait_ge(st[b], 16 * t)
                    v.tensor_tensor(YM[:, b, :, :], psY[:, :, :], SG[:, :, :], ALU.mult).then_inc(ym_ok, 1)
                    dve.wait_ge(ym_ok, n + 1)
            s.end(NT // 2, 18)


def merge_branches(pg):
    nc, i = pg.nc, pg.i
    m_d = pg.dram("mergedT", (KT, P, SEQ))
    HS = SEQ // 2
    with ExitStack() as c:
        sb = lambda n, s, d=F32: c.enter_context(nc.sbuf_tensor("b_" + n, s, d))
        sem = pg.semaphores(c, "b_")
        y_hi, y_lo = sb("y_hi", [P, 8, SEQ], F32R), sb("y_lo", [P, 8, SEQ], F32R)
        raw = sb("raw", [P, 2, 8, P])
        w_hi, w_lo = sb("w_hi", [P, 2, 8, P], F32R), sb("w_lo", [P, 2, 8, P], F32R)
        gt = sb("gate", [P, 2, 2, HS])
        o = sb("out", [P, 2, HS])
        ps = c.enter_context(nc.psum_tensor("b_ps", [P, 2, 2, HS], F32))
        y_in = [sem(f"y{k}") for k in range(4)]
        w_in = [sem(f"w{b}") for b in range(2)]
        g_in = [sem(f"g{b}") for b in range(2)]
        st = [pg.sw_sem(f"merge_stored{b}") for b in range(2)]
        y_h, y_l, wh_ok, wl_ok, mm, sg_ok, a_ok, o_ok = (sem(n) for n in ("yh", "yl", "wh", "wl", "mm", "sg", "a", "o"))
        yr = gt[:, :, :, :].rearrange("p a b n -> p (a b n)").rearrange("p (k n) -> p k n", n=SEQ)
        block = c.enter_context(nc.Block())

        @block.sync
        def _(sp):
            for k in range(8):
                if k >= 2:
                    sp.wait_ge(y_l, k - 1)
                src = pg.d["y_attT" if k < 4 else "y_mlT"]
                sp.dma_start(yr[:, k % 2, :], src[:, k % 4, :]).then_inc(y_in[k % 4], 16)
            sp.wait_ge(y_l, 8)
            with sp.Fori(0, KT // 2) as t:
                for b in range(2):
                    m = 2 * t + b
                    sp.wait_ge(wl_ok, 2 * t)
                    for k, name in ((0, "w_proj_att"), (1, "w_proj_mlstm")):
                        sp.dma_start(raw[:, b, 4 * k:4 * k + 4, :], i[name][:, bass.ds(m * P, P)].rearrange("(k p) n -> p k n", p=P)
                                     ).then_inc(w_in[b], 16)
                    for s in range(2):
                        sp.wait_ge(o_ok, 2 * m)
                        for k in range(2):
                            sp.dma_start(gt[:, s, k, :], pg.d["projT"][bass.ds(C_GA + k * DM + m * P, P), s * HS:(s + 1) * HS]
                                         ).then_inc(g_in[s], 16)

        @block.scalar
        def _(act):
            for k in range(8):
                act.wait_ge(y_in[k % 4], 16 * (k // 4 + 1))
                nc.scalar.copy(y_hi[:, k, :], yr[:, k % 2, :]).then_inc(y_h, 1)
            with act.Fori(0, KT // 2) as t:
                for b in range(2):
                    m = 2 * t + b
                    act.wait_ge(w_in[b], 32 * t + 32)
                    act.wait_ge(mm, 4 * t)
                    nc.scalar.copy(w_hi[:, b, :, :], raw[:, b, :, :]).then_inc(wh_ok, 1)
                    for s in range(2):
                        act.wait_ge(g_in[s], 32 * m + 32)
                        nc.scalar.activation(gt[:, s, :, :], gt[:, s, :, :], ACT.Sigmoid).then_inc(sg_ok, 1)

        @block.vector
        def _(dve):
            for k in range(8):
                dve.wait_ge(y_h, k + 1)
                nc.vector.tensor_tensor(y_lo[:, k, :], yr[:, k % 2, :], y_hi[:, k, :].bitcast(F32), ALU.subtract).then_inc(y_l, 1)
            with dve.Fori(0, KT // 2) as t:
                for b in range(2):
                    m = 2 * t + b
                    dve.wait_ge(wh_ok, m + 1)
                    nc.vector.tensor_tensor(w_lo[:, b, :, :], raw[:, b, :, :], w_hi[:, b, :, :].bitcast(F32), ALU.subtract).then_inc(wl_ok, 1)
                    for s in range(2):
                        dve.wait_ge(sg_ok, 2 * m + s + 1)
                        dve.wait_ge(mm, 2 * m + s + 1)
                        nc.vector.tensor_tensor(gt[:, s, :, :], ps[:, s, :, :], gt[:, s, :, :], ALU.mult).then_inc(a_ok, 1)
                        dve.wait_ge(a_ok, 2 * m + s + 1)
                        dve.wait_ge(st[s], 16 * m)
                        nc.vector.tensor_tensor(o[:, s, :], gt[:, s, 0, :], gt[:, s, 1, :], ALU.add).then_inc(o_ok, 1)

        @block.tensor
        def _(pe):
            pe.wait_ge(y_l, 8)
            with pe.Fori(0, KT // 2) as t:
                for b in range(2):
                    m = 2 * t + b
                    pe.wait_ge(wl_ok, m + 1)
                    for s in range(2):
                        pe.wait_ge(a_ok, 2 * m)
                        for br in range(2):
                            for k in range(4 * br, 4 * br + 4):
                                for r, (w, y) in enumerate(((w_hi, y_hi), (w_hi, y_lo), (w_lo, y_hi))):
                                    for q in range(2):
                                        at = s * HS + q * 512
                                        last = nc.tensor.matmul(ps[:, s, br, q * 512:(q + 1) * 512], w[:, b, k, :], y[:, k, at:at + 512],
                                                                start=(k == 4 * br and r == 0), stop=(k == 4 * br + 3 and r == 2))
                        last.then_inc(mm, 1)

        @block.gpsimd
        def _(pool):
            with pool.Fori(0, KT) as m:
                for s in range(2):
                    pool.wait_ge(o_ok, 2 * m + s + 1)
                    pool.dma_start(m_d[bass.ds(m, 1), :, s * HS:(s + 1) * HS].rearrange("o p n -> (o p) n"), o[:, s, :]).then_inc(st[s], 16)
            for s in range(2):
                pool.wait_ge(st[s], 16 * KT)


def output_and_router(pg):
    nc, i = pg.nc, pg.i
    x1_d, xn_d = pg.dram("x1", (SEQ, DM)), pg.dram("xn", (SEQ, DM))
    lg_d = pg.dram("router_logits", (P, NT, NG + NE))
    NR = NG + NE
    with ExitStack() as c:
        sb = lambda n, s, d=F32: c.enter_context(nc.sbuf_tensor("o_" + n, s, d))
        sem = pg.semaphores(c, "o_")
        raw = sb("raw", [P, 2, DM])
        w_hi, w_lo = sb("w_hi", [P, KT, DM], F32R), sb("w_lo", [P, KT, DM], F32R)
        M = sb("m", [P, 2, KT, P])
        m_hi, m_lo = sb("m_hi", [P, 2, KT, P], F32R), sb("m_lo", [P, 2, KT, P], F32R)
        X, XN, XT, SQ = sb("x", [P, 2, DM]), sb("xn", [P, 2, DM]), sb("xT", [P, 2, KT, P]), sb("sq", [P, DM])
        G = sb("gain", [P, DM])
        WR = sb("wr", [P, KT, NR])
        LG = sb("lg", [P, NT, NR])
        ss, rt, rs = (sb(n, [P, 2]) for n in ("ss", "rt", "rs"))
        eps, IDN = sb("eps", [P, 1]), sb("ident", [P, P])
        ps = c.enter_context(nc.psum_tensor("o_ps", [P, 2, DM], F32))
        pt = c.enter_context(nc.psum_tensor("o_pt", [P, KT, P], F32))
        pr = c.enter_context(nc.psum_tensor("o_pr", [P, 2, 512], F32))
        w_in = [sem(f"w{b}") for b in range(2)]
        m_in = [sem(f"m{b}") for b in range(2)]
        x_in = [sem(f"x{b}") for b in range(2)]
        st1 = [pg.sw_sem(f"x1_stored{b}") for b in range(2)]
        held = sem("held")
        stn = [pg.sw_sem(f"xn_stored{b}") for b in range(2)]
        (consts, setup, wh, wl, mh, ml, mm, x1_ok, sq_ok, rt_ok, rs_ok, xn_ok, tr, xt_ok, lg_ps, lg_ok, lg_st) = (sem(n) for n in (
            "consts", "setup", "wh", "wl", "mh", "ml", "mm", "x1_ok", "sq_ok", "rt_ok", "rs_ok", "xn_ok", "tr", "xt_ok", "lg_ps", "lg_ok", "lg_st"))
        block = c.enter_context(nc.Block())

        @block.sync
        def _(sp):
            for k in range(KT):
                if k >= 2:
                    sp.wait_ge(wl, k - 1)
                sp.dma_start(raw[:, k % 2, :], i["w_out"][k * P:(k + 1) * P, :]).then_inc(w_in[k % 2], 16)
            sp.dma_start(G[:, :], i["g_norm_moe"].partition_broadcast(P)).then_inc(consts, 16)
            sp.dma_start(WR[:, :, 0:NG], i["w_router_group"].rearrange("(k p) n -> p k n", p=P)).then_inc(consts, 16)
            sp.dma_start(WR[:, :, NG:NR], i["w_router_expert"].rearrange("(k p) n -> p k n", p=P)).then_inc(consts, 16)
            with sp.Fori(0, NT // 2) as t:
                for b in range(2):
                    n = 2 * t + b
                    sp.wait_ge(ml, 2 * t)
                    sp.dma_start(M[:, b, :, :], pg.d["mergedT"][:, :, bass.ds(n * P, P)].rearrange("k p n -> p k n")).then_inc(m_in[b], 16)
                for b in range(2):
                    n = 2 * t + b
                    sp.wait_ge(xn_ok, 2 * t)
                    hold(sp, held)
                    sp.wait_ge(st1[b], 16 * t)
                    sp.dma_start(X[:, b, :], i["x"][bass.ds(n * P, P), :]).then_inc(x_in[b], 16)
            sp.wait_ge(lg_ok, NT)
            sp.dma_start(lg_d, LG[:, :, :]).then_inc(lg_st, 16)
            sp.wait_ge(lg_st, 16)

        @block.gpsimd
        def _(pool):
            identity(nc, pool, IDN[:, :], setup)
            nc.gpsimd.memset(eps[:, :], EPS).then_inc(setup, 1)
            with pool.Fori(0, NT // 2) as t:
                for b in range(2):
                    rows = bass.ds((2 * t + b) * P, P)
                    pool.wait_ge(x1_ok, 2 * t + b + 1)
                    pool.dma_start(x1_d[rows, :], X[:, b, :]).then_inc(st1[b], 16)
                    pool.wait_ge(xn_ok, 2 * t + b + 1)
                    hold(pool, held)
                    pool.dma_start(xn_d[rows, :], XN[:, b, :]).then_inc(stn[b], 16)
            for b in range(2):
                pool.wait_ge(st1[b], 8 * NT)
                pool.wait_ge(stn[b], 8 * NT)

        @block.scalar
        def _(act):
            for k in range(KT):
                act.wait_ge(w_in[k % 2], 16 * (k // 2 + 1))
                nc.scalar.copy(w_hi[:, k, :], raw[:, k % 2, :]).then_inc(wh, 1)
            act.wait_ge(setup, 3)
            with act.Fori(0, NT // 2) as t:
                for b in range(2):
                    n = 2 * t + b
                    act.wait_ge(m_in[b], 16 * t + 16)
                    act.wait_ge(mm, 2 * t)
                    nc.scalar.copy(m_hi[:, b, :, :], M[:, b, :, :]).then_inc(mh, 1)
                for b in range(2):
                    n = 2 * t + b
                    act.wait_ge(x1_ok, n + 1)
                    act.wait_ge(sq_ok, n)
                    act.wait_ge(rs_ok, 2 * t)
                    nc.scalar.activation(SQ[:, :], X[:, b, :], ACT.Square, accum_out=ss[:, b:b + 1]).then_inc(sq_ok, 1)
                    act.wait_ge(sq_ok, n + 1)
                    nc.scalar.activation(rt[:, b:b + 1], ss[:, b:b + 1], ACT.Sqrt, bias=eps[:, :], scale=1.0 / DM).then_inc(rt_ok, 1)
                for b in range(2):
                    n = 2 * t + b
                    act.wait_ge(tr, n + 1)
                    act.wait_ge(lg_ps, 2 * t)
                    nc.scalar.copy(XT[:, b, :, :], pt[:, :, :]).then_inc(xt_ok, 1)

        @block.vector
        def _(dve):
            for k in range(KT):
                dve.wait_ge(wh, k + 1)
                nc.vector.tensor_tensor(w_lo[:, k, :], raw[:, k % 2, :], w_hi[:, k, :].bitcast(F32), ALU.subtract).then_inc(wl, 1)
            dve.wait_ge(consts, 48)
            with dve.Fori(0, NT // 2) as t:
                for b in range(2):
                    n = 2 * t + b
                    dve.wait_ge(mh, n + 1)
                    nc.vector.tensor_tensor(m_lo[:, b, :, :], M[:, b, :, :], m_hi[:, b, :, :].bitcast(F32), ALU.subtract).then_inc(ml, 1)
                for b in range(2):
                    n = 2 * t + b
                    dve.wait_ge(mm, n + 1)
                    dve.wait_ge(x_in[b], 16 * t + 16)
                    nc.vector.tensor_tensor(X[:, b, :], ps[:, b, :], X[:, b, :], ALU.add).then_inc(x1_ok, 1)
                for b in range(2):
                    n = 2 * t + b
                    dve.wait_ge(rt_ok, n + 1)
                    nc.vector.reciprocal(rs[:, b:b + 1], rt[:, b:b + 1]).then_inc(rs_ok, 1)
                    dve.wait_ge(rs_ok, n + 1)
                    dve.wait_ge(stn[b], 16 * t)
                    dve.wait_ge(tr, 2 * t)
                    nc.vector.scalar_tensor_tensor(out=XN[:, b, :], in0=X[:, b, :], scalar=rs[:, b:b + 1], in1=G[:, :],
                                                   op0=ALU.mult, op1=ALU.mult).then_inc(xn_ok, 1)
                for b in range(2):
                    n = 2 * t + b
                    dve.wait_ge(lg_ps, n + 1)
                    nc.vector.tensor_copy(LG[:, bass.ds(n, 1), :], pr[:, b:b + 1, 0:NR]).then_inc(lg_ok, 1)

        @block.tensor
        def _(pe):
            pe.wait_ge(wl, KT)
            pe.wait_ge(setup, 2)
            pe.wait_ge(consts, 48)
            with pe.Fori(0, NT // 2) as t:
                for b in range(2):
                    n = 2 * t + b
                    pe.wait_ge(ml, n + 1)
                    pe.wait_ge(x1_ok, 2 * t)
                    for k in range(KT):
                        for r, (m, w) in enumerate(((m_hi, w_hi), (m_hi, w_lo), (m_lo, w_hi))):
                            for q in range(2):
                                last = nc.tensor.matmul(ps[:, b, q * 512:(q + 1) * 512], m[:, b, k, :], w[:, k, q * 512:(q + 1) * 512],
                                                        start=(k == 0 and r == 0), stop=(k == KT - 1 and r == 2))
                    last.then_inc(mm, 1)
                for b in range(2):
                    n = 2 * t + b
                    pe.wait_ge(xn_ok, n + 1)
                    pe.wait_ge(xt_ok, n)
                    for k in range(KT):
                        last = nc.tensor.transpose(pt[:, k, :], XN[:, b, k * P:(k + 1) * P], IDN[:, :])
                    last.then_inc(tr, 1)
                    pe.wait_ge(xt_ok, n + 1)
                    pe.wait_ge(lg_ok, 2 * t)
                    for k in range(KT):
                        last = nc.tensor.matmul(pr[:, b, 0:NR], XT[:, b, k, :], WR[:, k, :], start=(k == 0), stop=(k == KT - 1))
                    last.then_inc(lg_ps, 1)


def route(pg):
    nc, i = pg.nc, pg.i
    NR = NG + NE
    tok_d = pg.dram("slot_token", (SLOTS + P, 1), I32)
    slot_d = pg.dram("slots", (P, 2, NT), I32)
    gate_d = pg.dram("gates", (P, 2, NT))
    be_d = pg.dram("block_expert", (1, EMPTY + 1), I32)
    with ExitStack() as c:
        sb = lambda n, s, d=F32: c.enter_context(nc.sbuf_tensor("r_" + n, s, d))
        sem = pg.semaphores(c, "r_")
        LG, BI = sb("lg", [P, NT, NR]), sb("bias", [P, 1, NR])
        gm, gs, ge = sb("gm", [P, NT, 1]), sb("gs", [P, NT, 1]), sb("ge", [P, NT, NG])
        og, pr4 = sb("og", [P, NT, NG]), sb("pr4", [P, NT, NG])
        sel, il, il2 = sb("sel", [P, NT, NG, EG]), sb("il", [P, NT, EG]), sb("il2", [P, NT, EG])
        m1, m2, mt = sb("m1", [P, NT, 1]), sb("m2", [P, NT, 1]), sb("mt", [P, NT, 1])
        o1, o2, pr8 = sb("o1", [P, NT, EG]), sb("o2", [P, NT, EG]), sb("pr8", [P, NT, EG])
        df, ex, dn = sb("df", [P, NT, 1]), sb("ex", [P, NT, 1]), sb("dn", [P, NT, 1])
        GA = sb("ga", [P, 2, NT])
        OH = sb("oh", [P, 2, NT, NE])
        OB = sb("ob", [P, NT, NE], BF16)
        lt, ones = sb("lt", [P, P], BF16), sb("ones", [P, P], BF16)
        rank, tot = sb("rank", [P, NT, NE]), sb("tot", [P, NT, NE])
        cum = sb("cum", [P, NT + 1, NE])
        nb, be, bs = sb("nb", [P, NE]), sb("be", [P, NE]), sb("bs", [P, 1, NE])
        T2 = sb("t2", [P, 2, NT, NE])
        SLf, SL = sb("slf", [P, 2, NT]), sb("sl", [P, 2, NT], I32)
        w4i, w8i, tki, bki = sb("w4i", [P, 1, NG], I32), sb("w8i", [P, 1, EG], I32), sb("tki", [P, NT], I32), sb("bki", [1, NBLK, 1], I32)
        w4, w8, bk = sb("w4", [P, 1, NG]), sb("w8", [P, 1, EG]), sb("bk", [1, NBLK, 1])
        le, ef = sb("le", [1, NBLK, NE]), sb("ef", [1, NBLK])
        ei = sb("ei", [1, EMPTY + 1], I32)
        zi = sb("zi", [P, NBLK + 1], I32)
        ps = c.enter_context(nc.psum_tensor("r_ps", [P, 2, NT * NE], F32))
        loads, setup, setup_d, own, ex_in, ex_ok, pe_in, pe_ok, out_ok, zst, st = (sem(n) for n in (
            "loads", "setup", "setup_d", "own", "ex_in", "ex_ok", "pe_in", "pe_ok", "out_ok", "zst", "st"))
        sc = pg.sw_sem("tokens_scattered")
        block = c.enter_context(nc.Block())

        @block.sync
        def _(sp):
            sp.dma_start(LG[:, :, :], pg.d["router_logits"]).then_inc(loads, 16)
            sp.dma_start(BI[:, 0, 0:NG], i["b_router_group"].partition_broadcast(P)).then_inc(loads, 16)
            sp.dma_start(BI[:, 0, NG:NR], i["b_router_expert"].partition_broadcast(P)).then_inc(loads, 16)
            sp.wait_ge(setup, 3)
            sp.dma_start(tok_d.rearrange("(p n) o -> p (n o)", p=P), zi[:, :]).then_inc(zst, 16)
            sp.wait_ge(out_ok, 1)
            sp.dma_start(slot_d, SL[:, :, :]).then_inc(st, 16)
            sp.dma_start(gate_d, GA[:, :, :]).then_inc(st, 16)
            sp.dma_start(be_d, ei[:, :]).then_inc(st, 16)
            sp.wait_ge(st, 48)

        @block.gpsimd
        def _(pool):
            nc.gpsimd.memset(lt[:, :], 1.0).then_inc(setup, 1)
            nc.gpsimd.memset(ones[:, :], 1.0)
            nc.gpsimd.memset(zi[:, :], 0)
            nc.gpsimd.iota(w4i[:, 0, :], [[-1, NG]], base=NG, channel_multiplier=0)
            nc.gpsimd.iota(w8i[:, 0, :], [[-1, EG]], base=EG, channel_multiplier=0)
            nc.gpsimd.iota(tki[:, :], [[P, NT]], base=0, channel_multiplier=1)
            nc.gpsimd.iota(bki[:, :, 0], [[1, NBLK]], base=0, channel_multiplier=0).then_inc(setup, 1)
            pool.wait_ge(setup, 1)
            nc.gpsimd.affine_select(out=lt[:, :], in_=lt[:, :], compare_op=ALU.is_gt, fill=0.0, base=0,
                                    pattern=[[1, P]], channel_multiplier=-1).then_inc(setup, 1)
            pool.wait_ge(out_ok, 1)
            pool.wait_ge(zst, 16)
            pool.wait_ge(setup, 3)
            for k in range(2):
                for t in range(NT):
                    pool.indirect_dma_start(tok_d, bass.IndirectOffsetOnAxis(SL[:, k, t:t + 1].bitcast(U32), 0), tki[:, t:t + 1], None).then_inc(sc, 16)
            pool.wait_ge(sc, 32 * NT)

        @block.scalar
        def _(act):
            act.wait_ge(ex_in, 1)
            nc.scalar.activation(ge[:, :, :], ge[:, :, :], ACT.Exp).then_inc(ex_ok, 1)
            act.wait_ge(ex_in, 2)
            nc.scalar.activation(ex[:, :, :], df[:, :, :], ACT.Exp).then_inc(ex_ok, 1)

        @block.vector
        def _(dve):
            s = Steps(dve, own)
            v = nc.vector
            dve.wait_ge(loads, 48)
            dve.wait_ge(setup, 3)
            v.tensor_copy(w4[:, :, :], w4i[:, :, :])
            v.tensor_copy(w8[:, :, :], w8i[:, :, :])
            v.tensor_copy(bk[:, :, :], bki[:, :, :])
            s(v.tensor_tensor(LG[:, :, :], LG[:, :, :], BI[:, :, :].broadcast_to([P, NT, NR]), ALU.add))
            gl = LG[:, :, 0:NG]

            def first_max(x, m, hot, pri, w):
                n = x.shape[2]
                s(v.tensor_reduce(m[:, :, 0], x, AX.X, ALU.max))
                s(v.tensor_tensor(pri, x, m.broadcast_to([P, NT, n]), ALU.is_equal))
                s(v.tensor_tensor(pri, pri, w.broadcast_to([P, NT, n]), ALU.mult))
                s(v.tensor_reduce(mt[:, :, 0], pri, AX.X, ALU.max))
                s(v.tensor_tensor(hot, pri, mt[:, :, :].broadcast_to([P, NT, n]), ALU.is_equal))

            first_max(gl, gm[:, :, :], og[:, :, :], pr4[:, :, :], w4[:, :, :])
            v.tensor_tensor(ge[:, :, :], gl, gm[:, :, :].broadcast_to([P, NT, NG]), ALU.subtract).then_inc(ex_in, 1)
            s(v.tensor_tensor(sel[:, :, :, :], LG[:, :, NG:NR].rearrange("p t (g e) -> p t g e", e=EG),
                              og[:, :, :].unsqueeze(3).broadcast_to([P, NT, NG, EG]), ALU.mult))
            s(v.tensor_reduce(il[:, :, :], sel[:, :, :, :].rearrange("p t g e -> p t e g"), AX.X, ALU.add))
            first_max(il[:, :, :], m1[:, :, :], o1[:, :, :], pr8[:, :, :], w8[:, :, :])
            s(v.scalar_tensor_tensor(out=il2[:, :, :], in0=o1[:, :, :], scalar=-3e38, in1=il[:, :, :], op0=ALU.mult, op1=ALU.add))
            first_max(il2[:, :, :], m2[:, :, :], o2[:, :, :], pr8[:, :, :], w8[:, :, :])
            v.tensor_tensor(df[:, :, :], m2[:, :, :], m1[:, :, :], ALU.subtract).then_inc(ex_in, 1)
            dve.wait_ge(ex_ok, 2)
            s(v.tensor_reduce(gs[:, :, 0], ge[:, :, :], AX.X, ALU.add))
            s(v.tensor_scalar(dn[:, :, :], ex[:, :, :], 1.0, None, ALU.add))
            s(v.tensor_tensor(dn[:, :, :], dn[:, :, :], gs[:, :, :], ALU.mult))
            s(v.reciprocal(GA[:, 0, :], dn[:, :, 0]))
            s(v.tensor_tensor(GA[:, 1, :], GA[:, 0, :], ex[:, :, 0], ALU.mult))
            for k, o in ((0, o1), (1, o2)):
                v.tensor_tensor(OH[:, k, :, :].rearrange("p t (g e) -> p t g e", e=EG), og[:, :, :].unsqueeze(3).broadcast_to([P, NT, NG, EG]),
                                o[:, :, :].unsqueeze(2).broadcast_to([P, NT, NG, EG]), ALU.mult)
            s(v.memset(cum[:, 0:1, :], 0.0))
            v.tensor_tensor(OB[:, :, :], OH[:, 0, :, :], OH[:, 1, :, :], ALU.add).then_inc(pe_in, 1)
            dve.wait_ge(pe_ok, 1)
            v.tensor_copy(rank[:, :, :], ps[:, 0, :].rearrange("p (t e) -> p t e", e=NE))
            s(v.tensor_copy(tot[:, :, :], ps[:, 1, :].rearrange("p (t e) -> p t e", e=NE)))
            for t in range(NT):
                s(v.tensor_tensor(cum[:, t + 1, :], cum[:, t, :], tot[:, t, :], ALU.add))
            s(v.tensor_tensor(rank[:, :, :], rank[:, :, :], cum[:, 0:NT, :], ALU.add))
            MAGIC = 12582912.0
            s(v.tensor_scalar(nb[:, :], cum[:, NT, :], float(P - 1), 1.0 / P, ALU.add, ALU.mult))
            s(v.tensor_scalar(nb[:, :], nb[:, :], -0.498, MAGIC, ALU.add, ALU.add))
            s(v.tensor_scalar(nb[:, :], nb[:, :], MAGIC, None, ALU.subtract))
            s(v.tensor_tensor_scan(be[:, :], nb[:, :], nb[:, :], 0.0, ALU.add, ALU.bypass))
            s(v.tensor_tensor(bs[:, 0, :], be[:, :], nb[:, :], ALU.subtract))
            s(v.tensor_scalar(bs[:, 0, :], bs[:, 0, :], float(P), None, ALU.mult))
            s(v.tensor_tensor(rank[:, :, :], rank[:, :, :], bs[:, :, :].broadcast_to([P, NT, NE]), ALU.add))
            for k in range(2):
                last = v.tensor_tensor(T2[:, k, :, :], OH[:, k, :, :], rank[:, :, :], ALU.mult)
            s(last)
            s(v.tensor_reduce(SLf[:, :, :], T2[:, :, :, :], AX.X, ALU.add))
            s(v.tensor_tensor(le[:, :, :], be[0:1, :].unsqueeze(1).broadcast_to([1, NBLK, NE]), bk[:, :, :].broadcast_to([1, NBLK, NE]), ALU.is_le))
            s(v.tensor_reduce(ef[:, :], le[:, :, :], AX.X, ALU.add))
            v.tensor_scalar(ei[:, 0:NBLK], ef[:, :], float(NE - 1), None, ALU.min)
            v.memset(ei[:, NBLK:USED], NE - 1)
            v.tensor_copy(ei[:, USED:USED + 1], be[0:1, NE - 1:NE])
            v.tensor_scalar(ei[:, LAST:LAST + 1], be[0:1, NE - 1:NE], -1.0, None, ALU.add)
            v.tensor_scalar(ei[:, EMPTY:EMPTY + 1], be[0:1, NE - 1:NE], -1.0, float(NBLK), ALU.mult, ALU.add)
            v.tensor_copy(SL[:, :, :], SLf[:, :, :]).then_inc(out_ok, 1)

        @block.tensor
        def _(pe):
            pe.wait_ge(setup, 3)
            pe.wait_ge(pe_in, 1)
            nc.tensor.matmul(ps[:, 0, :], lt[:, :], OB[:, :, :].rearrange("p t e -> p (t e)"), start=True, stop=True)
            nc.tensor.matmul(ps[:, 1, :], ones[:, :], OB[:, :, :].rearrange("p t e -> p (t e)"), start=True, stop=True).then_inc(pe_ok, 1)


def experts(pg):
    nc, i = pg.nc, pg.i
    yb_d = pg.dram("slot_out", (SLOTS, DM))
    KH = DE // P
    NU = KT + KH
    with ExitStack() as c:
        sb = lambda n, s, d=F32: c.enter_context(nc.sbuf_tensor("e_" + n, s, d))
        sem = pg.semaphores(c, "e_")
        raw = sb("raw", [P, NU, 1024])
        w_hi, w_lo = sb("w_hi", [P, NU, 1024], F32R), sb("w_lo", [P, NU, 1024], F32R)
        IX = sb("ix", [P, 1], I32)
        XG = sb("xg", [P, DM])
        x_hi, x_lo = sb("x_hi", [P, KT, P], F32R), sb("x_lo", [P, KT, P], F32R)
        SG, H = sb("sg", [P, DE]), sb("h", [P, DE])
        h_hi, h_lo = sb("h_hi", [P, KH, P], F32R), sb("h_lo", [P, KH, P], F32R)
        Y = sb("y", [P, DM])
        BE = sb("be", [1, EMPTY + 1], I32)
        Z = sb("zeros", [P, DM])
        IDN = sb("ident", [P, P])
        psX = c.enter_context(nc.psum_tensor("e_pX", [P, KT, P], F32))
        psG = c.enter_context(nc.psum_tensor("e_pG", [P, 2, DE], F32))
        psH = c.enter_context(nc.psum_tensor("e_pH", [P, KH, P], F32))
        psY = c.enter_context(nc.psum_tensor("e_pY", [P, DM], F32))
        w_in = [sem(f"w{u}") for u in range(NU)]
        held, z_st = sem("held"), sem("zeros_stored")
        EARLY = KT - 2
        (be_in, setup, gh, gl, dh, dl, xt_ps, xh_ok, xl_ok, gu_ps, sg_ok, h_ok, ht_ps, hh_ok, hl_ok, y_ps, ya_ok, yv_ok) = (
            sem(n) for n in ("be_in", "setup", "gate_up_hi", "gate_up_lo", "down_hi", "down_lo", "xt_ps", "xh_ok", "xl_ok", "gu_ps", "sg_ok", "h_ok", "ht_ps",
                             "hh_ok", "hl_ok", "y_ps", "ya_ok", "yv_ok"))
        ix_in, x_in, y_st = (pg.sw_sem("e_" + n) for n in ("ix_in", "x_in", "y_st"))
        block = c.enter_context(nc.Block())
        wg, wu, wd = i["w_exp_gate"], i["w_exp_up"], i["w_exp_down"]

        def blocks_in_use(eng):
            eng.wait_ge(be_in, 16)
            return (eng.value_load(BE[0:1, USED:USED + 1], min_val=2 * NT, max_val=NBLK),
                    eng.value_load(BE[0:1, LAST:LAST + 1], min_val=2 * NT - 1, max_val=NBLK - 1))

        @block.sync
        def _(sp):
            sp.dma_start(BE[:, :], pg.d["block_expert"]).then_inc(be_in, 16)
            used, end = blocks_in_use(sp)
            sp.wait_ge(setup, 3)
            sp.sem_inc(z_st, 16)

            def load_gate_up(e, cond, last=None):
                for u in range(KT):
                    if last is not None:
                        sp.wait_ge(gl, last * KT + (u + 1))
                        hold(sp, held)
                    sp.dma_start(raw[:, u, 0:DE], wg[bass.ds(e, 1), u * P:(u + 1) * P, :].rearrange("o p n -> (o p) n"), **cond).then_inc(w_in[u], 16)
                    sp.dma_start(raw[:, u, DE:2 * DE], wu[bass.ds(e, 1), u * P:(u + 1) * P, :].rearrange("o p n -> (o p) n"), **cond).then_inc(w_in[u], 16)

            def load_down(e, cond, last=None):
                for k in range(KH):
                    if last is not None:
                        sp.wait_ge(dl, last * KH + (k + 1))
                        hold(sp, held)
                    sp.dma_start(raw[:, KT + k, :], wd[bass.ds(e, 1), k * P:(k + 1) * P, :].rearrange("o p n -> (o p) n"), **cond).then_inc(w_in[KT + k], 16)

            def expert(n):
                return sp.value_load(BE[0:1, bass.ds(n, 1)], min_val=0, max_val=NE - 1)
            e0, e1 = expert(0), expert(1)
            load_gate_up(e0, {})
            load_down(e0, {})
            load_gate_up(e1, dict(cond=e1 != e0), 0)
            with sp.Fori(1, NBLK) as n:
                with sp.If(n < used):
                    before, this, after = expert(n - 1), expert(n), expert(n + 1)
                    load_gate_up(after, dict(cond=after != this), n)
                    load_down(this, dict(cond=this != before), n - 1)
                with sp.If(n >= used):
                    sp.dma_start(yb_d[bass.ds(n * P, P), :], Z[:, :]).then_inc(z_st, 16)
            empty = sp.value_load(BE[0:1, EMPTY:EMPTY + 1], min_val=0, max_val=NBLK - 2 * NT)
            sp.wait_ge(z_st, 16 * empty + 16)
            hold(sp, held)
            for u in range(KT):
                sp.wait_ge(w_in[u], 32 * used + 32)
                hold(sp, held)
            for k in range(KH):
                sp.wait_ge(w_in[KT + k], 16 * used)
                hold(sp, held)

        @block.gpsimd
        def _(pool):
            identity(nc, pool, IDN[:, :], setup)
            nc.gpsimd.memset(Z[:, :], 0.0).then_inc(setup, 1)
            used, end = blocks_in_use(pool)

            def gather(n):
                pool.dma_start(IX[:, :], pg.d["slot_token"][bass.ds(n * P, P), :]).then_inc(ix_in, 16)
                pool.wait_ge(ix_in, 16 * n + 16)
                hold(pool, held)
                pool.indirect_dma_start(XG[:, :], None, pg.d["xn"], bass.IndirectOffsetOnAxis(IX[:, 0:1].bitcast(U32), 0)).then_inc(x_in, 16)

            def store(n):
                pool.wait_ge(ya_ok, n + 1)
                pool.wait_ge(yv_ok, n + 1)
                pool.dma_start(yb_d[bass.ds(n * P, P), :], Y[:, :]).then_inc(y_st, 16)
            gather(0)
            pool.wait_ge(x_in, 16)
            pool.wait_ge(xt_ps, 1)
            gather(1)
            with pool.Fori(1, NBLK) as n:
                with pool.If(n < used):
                    pool.wait_ge(x_in, 16 * n + 16)
                    pool.wait_ge(xt_ps, n + 1)
                    gather(n + 1)
                    store(n - 1)
            store(end)
            pool.wait_ge(x_in, 16 * used + 16)
            pool.wait_ge(y_st, 16 * used)

        @block.tensor
        def _(pe):
            used, end = blocks_in_use(pe)
            pe.wait_ge(setup, 2)

            def rows_t(n):
                pe.wait_ge(x_in, 16 * n + 16)
                pe.wait_ge(xl_ok, n)
                for k in range(KT):
                    last = nc.tensor.transpose(psX[:, k, :], XG[:, k * P:(k + 1) * P], IDN[:, :])
                last.then_inc(xt_ps, 1)

            def gate_up(n):
                pe.wait_ge(xl_ok, n + 1)
                pe.wait_ge(h_ok, n)
                for k in range(KT):
                    pe.wait_ge(gl, n * KT + (k + 1))
                    for r, (x, w) in enumerate(((x_hi, w_hi), (x_hi, w_lo), (x_lo, w_hi))):
                        for q in range(2):
                            last = nc.tensor.matmul(psG[:, q, :], x[:, k, :], w[:, k, q * DE:(q + 1) * DE],
                                                    start=(k == 0 and r == 0), stop=(k == KT - 1 and r == 2))
                    last.then_inc(gu_ps, 1)

            def hidden_t(n):
                pe.wait_ge(h_ok, n + 1)
                for k in range(KH):
                    last = nc.tensor.transpose(psH[:, k, :], H[:, k * P:(k + 1) * P], IDN[:, :])
                last.then_inc(ht_ps, 1)

            def down(n):
                pe.wait_ge(hl_ok, n + 1)
                pe.wait_ge(ya_ok, n)
                pe.wait_ge(yv_ok, n)
                for k in range(KH):
                    pe.wait_ge(dl, n * KH + (k + 1))
                    for r, (h, w) in enumerate(((h_hi, w_hi), (h_hi, w_lo), (h_lo, w_hi))):
                        for q in range(2):
                            last = nc.tensor.matmul(psY[:, q * 512:(q + 1) * 512], h[:, k, :], w[:, KT + k, q * 512:(q + 1) * 512],
                                                    start=(k == 0 and r == 0), stop=(k == KH - 1 and r == 2))
                last.then_inc(y_ps, 1)
            rows_t(0)
            gate_up(0)
            rows_t(1)
            with pe.Fori(1, NBLK) as n:
                with pe.If(n < used):
                    hidden_t(n - 1)
                    gate_up(n)
                    rows_t(n + 1)
                    down(n - 1)
            hidden_t(end)
            down(end)

        @block.scalar
        def _(act):
            used, end = blocks_in_use(act)

            def rows(n):
                act.wait_ge(xt_ps, n + 1)
                act.wait_ge(gu_ps, n * KT)
                nc.scalar.copy(x_hi[:, :, :], psX[:, :, :]).then_inc(xh_ok, 1)

            def gate_up_weights(n, lo, hi, first=False):
                for u in range(lo, hi):
                    act.wait_ge(w_in[u], 32 * n + 32)
                    if not first:
                        act.wait_ge(gu_ps, (n - 1) * KT + (u + 1))
                    nc.scalar.copy(w_hi[:, u, :], raw[:, u, :]).then_inc(gh, 1)

            def gate(n):
                act.wait_ge(gu_ps, n * KT + KT)
                act.wait_ge(h_ok, n)
                nc.scalar.activation(SG[:, :], psG[:, 0, :], ACT.Silu).then_inc(sg_ok, 1)

            def down_operands(n):
                act.wait_ge(ht_ps, n + 1)
                act.wait_ge(y_ps, n)
                nc.scalar.copy(h_hi[:, :, :], psH[:, :, :]).then_inc(hh_ok, 1)
                for k in range(KH):
                    act.wait_ge(w_in[KT + k], 16 * n + 16)
                    nc.scalar.copy(w_hi[:, KT + k, :], raw[:, KT + k, :]).then_inc(dh, 1)

            def result(n):
                act.wait_ge(y_ps, n + 1)
                act.wait_ge(y_st, 16 * n)
                nc.scalar.copy(Y[:, 0:512], psY[:, 0:512]).then_inc(ya_ok, 1)
            act.wait_ge(xt_ps, 1)
            nc.scalar.copy(x_hi[:, :, :], psX[:, :, :]).then_inc(xh_ok, 1)
            gate_up_weights(0, 0, KT, first=True)
            gate_up_weights(1, 0, EARLY)
            gate(0)
            rows(1)
            gate_up_weights(1, EARLY, KT)
            with act.Fori(1, NBLK) as n:
                with act.If(n < used):
                    down_operands(n - 1)
                    gate_up_weights(n + 1, 0, EARLY)
                    gate(n)
                    rows(n + 1)
                    gate_up_weights(n + 1, EARLY, KT)
                    result(n - 1)
            down_operands(end)
            result(end)

        @block.vector
        def _(dve):
            used, end = blocks_in_use(dve)

            def rows(n):
                dve.wait_ge(xh_ok, n + 1)
                nc.vector.tensor_tensor(x_lo[:, :, :], psX[:, :, :], x_hi[:, :, :].bitcast(F32), ALU.subtract).then_inc(xl_ok, 1)

            def gate_up_weights(n, lo, hi):
                for u in range(lo, hi):
                    dve.wait_ge(gh, n * KT + (u + 1))
                    nc.vector.tensor_tensor(w_lo[:, u, :], raw[:, u, :], w_hi[:, u, :].bitcast(F32), ALU.subtract).then_inc(gl, 1)

            def hidden(n):
                dve.wait_ge(sg_ok, n + 1)
                dve.wait_ge(ht_ps, n)
                nc.vector.tensor_tensor(H[:, :], psG[:, 1, :], SG[:, :], ALU.mult).then_inc(h_ok, 1)

            def down_operands(n):
                dve.wait_ge(hh_ok, n + 1)
                nc.vector.tensor_tensor(h_lo[:, :, :], psH[:, :, :], h_hi[:, :, :].bitcast(F32), ALU.subtract).then_inc(hl_ok, 1)
                for k in range(KH):
                    dve.wait_ge(dh, n * KH + (k + 1))
                    nc.vector.tensor_tensor(w_lo[:, KT + k, :], raw[:, KT + k, :], w_hi[:, KT + k, :].bitcast(F32), ALU.subtract).then_inc(dl, 1)

            def result(n):
                dve.wait_ge(y_ps, n + 1)
                dve.wait_ge(y_st, 16 * n)
                nc.vector.tensor_copy(Y[:, 512:], psY[:, 512:]).then_inc(yv_ok, 1)
            rows(0)
            gate_up_weights(0, 0, KT)
            gate_up_weights(1, 0, EARLY)
            hidden(0)
            rows(1)
            gate_up_weights(1, EARLY, KT)
            with dve.Fori(1, NBLK) as n:
                with dve.If(n < used):
                    down_operands(n - 1)
                    gate_up_weights(n + 1, 0, EARLY)
                    hidden(n)
                    rows(n + 1)
                    gate_up_weights(n + 1, EARLY, KT)
                    result(n - 1)
            down_operands(end)
            result(end)


def combine(pg):
    nc = pg.nc
    with ExitStack() as c:
        sb = lambda n, s, d=F32: c.enter_context(nc.sbuf_tensor("c_" + n, s, d))
        sem = pg.semaphores(c, "c_")
        SL, GA = sb("sl", [P, 2, NT], I32), sb("ga", [P, 2, NT])
        X, Y = sb("x", [P, 4, DM]), sb("y", [P, 4, 2, DM])
        consts, a_ok, o_ok = sem("consts"), sem("a"), sem("o")
        x_in = [sem(f"x{b}") for b in range(4)]
        y_in = [pg.sw_sem(f"y_gathered{b}") for b in range(4)]
        st = [sem(f"st{b}") for b in range(4)]
        block = c.enter_context(nc.Block())

        @block.sync
        def _(sp):
            sp.dma_start(SL[:, :, :], pg.d["slots"]).then_inc(consts, 16)
            sp.dma_start(GA[:, :, :], pg.d["gates"]).then_inc(consts, 16)
            for t in range(NT):
                if t >= 4:
                    sp.wait_ge(st[t % 4], 16 * (t // 4))
                sp.dma_start(X[:, t % 4, :], pg.d["x1"][t * P:(t + 1) * P, :]).then_inc(x_in[t % 4], 16)

        @block.gpsimd
        def _(pool):
            pool.wait_ge(consts, 32)
            for t in range(NT):
                if t >= 4:
                    pool.wait_ge(o_ok, t - 3)
                for k in range(2):
                    pool.indirect_dma_start(Y[:, t % 4, k, :], None, pg.d["slot_out"], bass.IndirectOffsetOnAxis(SL[:, k, t:t + 1].bitcast(U32), 0)
                                            ).then_inc(y_in[t % 4], 16)

        @block.vector
        def _(dve):
            dve.wait_ge(consts, 32)
            for t in range(NT):
                b = t % 4
                dve.wait_ge(x_in[b], 16 * (t // 4 + 1))
                dve.wait_ge(y_in[b], 32 * (t // 4 + 1))
                nc.vector.scalar_tensor_tensor(out=X[:, b, :], in0=Y[:, b, 0, :], scalar=GA[:, 0, t:t + 1], in1=X[:, b, :],
                                               op0=ALU.mult, op1=ALU.add).then_inc(a_ok, 1)
                dve.wait_ge(a_ok, t + 1)
                nc.vector.scalar_tensor_tensor(out=X[:, b, :], in0=Y[:, b, 1, :], scalar=GA[:, 1, t:t + 1], in1=X[:, b, :],
                                               op0=ALU.mult, op1=ALU.add).then_inc(o_ok, 1)

        @block.scalar
        def _(act):
            for t in range(NT):
                act.wait_ge(o_ok, t + 1)
                act.dma_start(pg.out[t * P:(t + 1) * P, :], X[:, t % 4, :]).then_inc(st[t % 4], 16)
            for b in range(4):
                act.wait_ge(st[b], 16 * (NT // 4))


def layout(a):
    out = {n: np.ascontiguousarray(v[0]) for n, v in a.items()}
    out["positions"] = np.ascontiguousarray(out["positions"].reshape(NT, P).T)
    out["b_igate"] = np.repeat(out["b_igate"], NT).reshape(MH * NT, 1)
    out["b_fgate"] = np.repeat(out["b_fgate"], NT).reshape(MH * NT, 1)
    out["w_conv_mlstm"] = np.ascontiguousarray(out["w_conv_mlstm"].reshape(CONV, 2 * MH, P).transpose(2, 0, 1))
    out["b_conv_mlstm"] = np.ascontiguousarray(out["b_conv_mlstm"].reshape(2 * MH, P).T)
    return out


def build(nc, ins, out):
    pg = Prog(nc, ins)
    pg.out = out
    for stage in (project_in, attention_operands, sparse_attention, mlstm_gates, mlstm_conv, mlstm_scan, merge_branches,
                  output_and_router, route, experts, combine):
        stage(pg)


def kernel(**inputs):
    import concourse.bacc as bacc
    from concourse.bass_utils import run_bass_kernel_spmd

    nc = bacc.Bacc("TRN2", target_bir_lowering=False, num_devices=1)
    arrays, ins = {}, {}
    for name, a in layout({n: np.asarray(v) for n, v in inputs.items()}).items():
        arrays["in_" + name] = a
        ins[name] = nc.dram_tensor("in_" + name, a.shape, mybir.dt.from_np(a.dtype), kind="ExternalInput").ap()
    out = nc.dram_tensor("out_0_dram", (SEQ, DM), F32, kind="ExternalOutput").ap()
    build(nc, ins, out)
    r = run_bass_kernel_spmd(nc, [arrays], core_ids=[0])
    return r.results[0]["out_0_dram"].reshape(1, SEQ, DM)
```
